# Optimizing a Trainium2 kernel written in Bass

```python
import math
import jax
import jax.numpy as jnp
from jax import lax
import numpy as np
import jax, jax.numpy as jnp

D_MODEL = 1024
BATCH = 1
SEQ = 256
DEPTH = 2

CTX_LEN = 256
GRID_W = 64
HEAD_DIM = 64
MIX_W = D_MODEL
A_HEADS = D_MODEL // (4 * HEAD_DIM)
A_DK = HEAD_DIM // 2
A_DV = HEAD_DIM
A_W = A_HEADS * HEAD_DIM
B_HEADS = 3 * D_MODEL // (8 * HEAD_DIM)
B_KV_HEADS = 2
B_W = B_HEADS * HEAD_DIM
B_KV_W = B_KV_HEADS * HEAD_DIM
C_HEADS = 3 * D_MODEL // (8 * HEAD_DIM)
C_W = C_HEADS * HEAD_DIM
WIN_H = 8
WIN_W = 16
Q_BLOCK = 128
ROPE_THETA = 10000.0
EPS = 1e-6
SPLIT_SIZES = (A_W, A_W, A_W, A_W, B_W, B_KV_W, B_KV_W, B_W, C_W, C_W, C_W, C_W)
IN_W = sum(SPLIT_SIZES)


def rms_norm(x, g):
    xf = x.astype(jnp.float32)
    y = xf * lax.rsqrt(jnp.mean(xf * xf, axis=-1, keepdims=True) + EPS)
    return (y * g.astype(jnp.float32)).astype(x.dtype)

def axial_rope(x, row, col):
    d = x.shape[-1]
    nf = d // 4
    inv = ROPE_THETA ** (-jnp.arange(nf, dtype=jnp.float32) / nf)
    ang = jnp.concatenate([row[:, None] * inv, col[:, None] * inv], axis=-1)
    shape = (1, x.shape[1]) + (1,) * (x.ndim - 3) + (d // 2,)
    cos = jnp.cos(ang).reshape(shape)
    sin = jnp.sin(ang).reshape(shape)
    xf = x.astype(jnp.float32)
    x1, x2 = xf[..., : d // 2], xf[..., d // 2:]
    return jnp.concatenate([x1 * cos - x2 * sin, x2 * cos + x1 * sin], axis=-1).astype(x.dtype)

def map_query_blocks(fn, q):
    b, s = q.shape[:2]
    nb = s // Q_BLOCK
    qb = jnp.moveaxis(q.reshape((b, nb, Q_BLOCK) + q.shape[2:]), 1, 0)
    out = lax.map(fn, qb)
    return jnp.moveaxis(out, 0, 1).reshape((b, s) + out.shape[3:])

def diff_attend(q, k, v, lam):
    s = jnp.einsum('bqhmd,bkhmd->bhmqk', q, k).astype(jnp.float32) * (q.shape[-1] ** -0.5)
    p = jax.nn.softmax(s, axis=-1)
    a = (p[:, :, 0] - lam * p[:, :, 1]).astype(v.dtype)
    return jnp.einsum('bhqk,bkhd->bqhd', a, v)

def gqa_attend(q, k, v):
    b, nq, h, d = q.shape
    kvh = k.shape[2]
    qg = q.reshape(b, nq, kvh, h // kvh, d)
    s = jnp.einsum('bqhgd,bkhd->bhgqk', qg, k).astype(jnp.float32) * (d ** -0.5)
    p = jax.nn.softmax(s, axis=-1).astype(v.dtype)
    o = jnp.einsum('bhgqk,bkhd->bqhgd', p, v)
    return o.reshape(b, nq, h * v.shape[-1])

def neighbourhood_attend(q, k, v, k_ctx, v_ctx, rpb, rows):
    b, s, h, d = q.shape
    kh = min(WIN_H, rows)
    kw = WIN_W
    scale = d ** -0.5
    qg = q.reshape(b, rows, GRID_W, h, d)
    kg = k.reshape(b, rows, GRID_W, h, d)
    vg = v.reshape(b, rows, GRID_W, h, d)
    r = jnp.arange(rows)
    cidx = jnp.arange(GRID_W)
    r0 = jnp.clip(r - kh // 2, 0, rows - kh)
    key_rows = r0[:, None] + jnp.arange(kh)
    k_blk = kg[:, key_rows]
    v_blk = vg[:, key_rows]
    c0 = jnp.clip(cidx - kw // 2, 0, GRID_W - kw)
    in_win = (cidx[None, :] >= c0[:, None]) & (cidx[None, :] < c0[:, None] + kw)
    dr = key_rows - r[:, None] + (WIN_H - 1)
    dc = jnp.clip(cidx[None, :] - cidx[:, None] + (WIN_W - 1), 0, 2 * WIN_W - 2)
    bias = rpb[:, dr[:, None, :, None], dc[None, :, None, :]]
    s_nb = jnp.einsum('brqhd,brkwhd->bhrqkw', qg, k_blk).astype(jnp.float32) * scale
    s_nb = s_nb + bias.astype(jnp.float32)[None]
    s_nb = jnp.where(in_win[:, None, :], s_nb, -jnp.inf)
    s_cx = jnp.einsum('brqhd,bchd->bhrqc', qg, k_ctx).astype(jnp.float32) * scale
    n_nb = kh * GRID_W
    sc = jnp.concatenate([s_nb.reshape(b, h, rows, GRID_W, n_nb), s_cx], axis=-1)
    p = jax.nn.softmax(sc, axis=-1).astype(v.dtype)
    p_nb = p[..., :n_nb].reshape(b, h, rows, GRID_W, kh, GRID_W)
    p_cx = p[..., n_nb:]
    o = jnp.einsum('bhrqkw,brkwhd->brqhd', p_nb, v_blk) + jnp.einsum('bhrqc,bchd->brqhd', p_cx, v_ctx)
    return o.reshape(b, s, h * d)

def split_proj(p):
    idx = np.cumsum(SPLIT_SIZES)[:-1].tolist()
    return jnp.split(p, idx, axis=-1)

def first_inputs(seed: int = 0) -> dict:
    key = jax.random.key(seed)
    ks = jax.random.split(key, 22)
    nrm = jax.random.normal
    f32 = jnp.float32
    return {
        'x': nrm(ks[0], (BATCH, SEQ, D_MODEL), f32),
        'c': nrm(ks[1], (BATCH, D_MODEL), f32),
        'ctx': nrm(ks[2], (BATCH, CTX_LEN, D_MODEL), f32),
        'c_ctx': nrm(ks[3], (D_MODEL,), f32),
        'norm_g': 1.0 + 0.05 * nrm(ks[4], (DEPTH, D_MODEL), f32),
        'w_ada': nrm(ks[5], (DEPTH, D_MODEL, 3 * D_MODEL), f32) * (0.5 * D_MODEL ** -0.5),
        'b_ada': 0.01 * nrm(ks[6], (DEPTH, 3 * D_MODEL), f32),
        'w_in': nrm(ks[7], (DEPTH, D_MODEL, IN_W), f32) * (D_MODEL ** -0.5),
        'w_out': nrm(ks[8], (DEPTH, MIX_W, D_MODEL), f32) * (MIX_W ** -0.5),
        'diff_q_norm': 1.0 + 0.05 * nrm(ks[9], (DEPTH, A_DK), f32),
        'diff_k_norm': 1.0 + 0.05 * nrm(ks[10], (DEPTH, A_DK), f32),
        'lambda_q1': 0.1 * nrm(ks[11], (DEPTH, A_DK), f32),
        'lambda_k1': 0.1 * nrm(ks[12], (DEPTH, A_DK), f32),
        'lambda_q2': 0.1 * nrm(ks[13], (DEPTH, A_DK), f32),
        'lambda_k2': 0.1 * nrm(ks[14], (DEPTH, A_DK), f32),
        'diff_subln': 1.0 + 0.05 * nrm(ks[15], (DEPTH, A_DV), f32),
        'gqa_q_norm': 1.0 + 0.05 * nrm(ks[16], (DEPTH, HEAD_DIM), f32),
        'gqa_k_norm': 1.0 + 0.05 * nrm(ks[17], (DEPTH, HEAD_DIM), f32),
        'nat_q_norm': 1.0 + 0.05 * nrm(ks[18], (DEPTH, HEAD_DIM), f32),
        'nat_k_norm': 1.0 + 0.05 * nrm(ks[19], (DEPTH, HEAD_DIM), f32),
        'nat_rpb': 0.1 * nrm(ks[20], (DEPTH, C_HEADS, 2 * WIN_H - 1, 2 * WIN_W - 1), f32),
    }

def first_block(x, c, ctx, c_ctx, norm_g, w_ada, b_ada, w_in, w_out, diff_q_norm, diff_k_norm,
              lambda_q1, lambda_k1, lambda_q2, lambda_k2, diff_subln, gqa_q_norm, gqa_k_norm,
              nat_q_norm, nat_k_norm, nat_rpb):
    b, s, _ = x.shape
    n_ctx = ctx.shape[1]
    rows = s // GRID_W
    t = jnp.arange(s)
    row = (t // GRID_W).astype(jnp.float32)
    col = (t % GRID_W).astype(jnp.float32)
    for l in range(DEPTH):
        lam_init = 0.8 - 0.6 * math.exp(-0.3 * l)
        sh, sc, gt = jnp.split(jax.nn.silu(c) @ w_ada[l] + b_ada[l], 3, axis=-1)
        sh_c, sc_c, gt_c = jnp.split(jax.nn.silu(c_ctx) @ w_ada[l] + b_ada[l], 3, axis=-1)
        h = rms_norm(x, norm_g[l]) * (1 + sc[:, None]) + sh[:, None]
        hc = rms_norm(ctx, norm_g[l]) * (1 + sc_c) + sh_c
        qa, ka, va, ga, qb, kb, vb, gb, qn, kn, vn, gn = split_proj(h @ w_in[l])
        qa_c, ka_c, va_c, ga_c, qb_c, kb_c, vb_c, gb_c, qn_c, kn_c, vn_c, gn_c = split_proj(hc @ w_in[l])

        lam = (jnp.exp(jnp.sum(lambda_q1[l] * lambda_k1[l])) - jnp.exp(jnp.sum(lambda_q2[l] * lambda_k2[l]))
               + lam_init).astype(jnp.float32)
        qa = axial_rope(rms_norm(qa.reshape(b, s, A_HEADS, 2, A_DK), diff_q_norm[l]), row, col)
        ka = axial_rope(rms_norm(ka.reshape(b, s, A_HEADS, 2, A_DK), diff_k_norm[l]), row, col)
        ka_c = rms_norm(ka_c.reshape(b, n_ctx, A_HEADS, 2, A_DK), diff_k_norm[l])
        va_c = va_c.reshape(b, n_ctx, A_HEADS, A_DV)
        ka_all = jnp.concatenate([ka, ka_c], axis=1)
        va_all = jnp.concatenate([va.reshape(b, s, A_HEADS, A_DV), va_c], axis=1)
        oa = map_query_blocks(lambda q_blk: diff_attend(q_blk, ka_all, va_all, lam), qa)
        ya = (rms_norm(oa, diff_subln[l]) * (1 - lam_init)).reshape(b, s, A_W) * jax.nn.silu(ga)

        qb = axial_rope(rms_norm(qb.reshape(b, s, B_HEADS, HEAD_DIM), gqa_q_norm[l]), row, col)
        kb = axial_rope(rms_norm(kb.reshape(b, s, B_KV_HEADS, HEAD_DIM), gqa_k_norm[l]), row, col)
        kb_c = rms_norm(kb_c.reshape(b, n_ctx, B_KV_HEADS, HEAD_DIM), gqa_k_norm[l])
        vb_c = vb_c.reshape(b, n_ctx, B_KV_HEADS, HEAD_DIM)
        kb_all = jnp.concatenate([kb, kb_c], axis=1)
        vb_all = jnp.concatenate([vb.reshape(b, s, B_KV_HEADS, HEAD_DIM), vb_c], axis=1)
        yb = map_query_blocks(lambda q_blk: gqa_attend(q_blk, kb_all, vb_all), qb) * jax.nn.silu(gb)

        qn = rms_norm(qn.reshape(b, s, C_HEADS, HEAD_DIM), nat_q_norm[l])
        kn = rms_norm(kn.reshape(b, s, C_HEADS, HEAD_DIM), nat_k_norm[l])
        kn_c = rms_norm(kn_c.reshape(b, n_ctx, C_HEADS, HEAD_DIM), nat_k_norm[l])
        vn_c = vn_c.reshape(b, n_ctx, C_HEADS, HEAD_DIM)
        yn = neighbourhood_attend(qn, kn, vn.reshape(b, s, C_HEADS, HEAD_DIM), kn_c, vn_c, nat_rpb[l], rows)
        yn = yn * jax.nn.silu(gn)

        y = jnp.concatenate([ya, yb, yn], axis=-1) @ w_out[l]

        if l < DEPTH - 1:
            qa_c = rms_norm(qa_c.reshape(b, n_ctx, A_HEADS, 2, A_DK), diff_q_norm[l])
            oa_c = diff_attend(qa_c, ka_c, va_c, lam)
            ya_c = (rms_norm(oa_c, diff_subln[l]) * (1 - lam_init)).reshape(b, n_ctx, A_W) * jax.nn.silu(ga_c)
            qb_c = rms_norm(qb_c.reshape(b, n_ctx, B_HEADS, HEAD_DIM), gqa_q_norm[l])
            yb_c = gqa_attend(qb_c, kb_c, vb_c) * jax.nn.silu(gb_c)
            qn_c = rms_norm(qn_c.reshape(b, n_ctx, C_HEADS, HEAD_DIM), nat_q_norm[l])
            yn_c = gqa_attend(qn_c, kn_c, vn_c) * jax.nn.silu(gn_c)
            ctx = ctx + gt_c * (jnp.concatenate([ya_c, yb_c, yn_c], axis=-1) @ w_out[l])

        x = x + gt[:, None] * y
    return x


N_MIXERS = 2
RMS_EPS = 1e-6
LN_EPS = 1e-5

GMLP_EXPAND = 2
GMLP_WIDTH = GMLP_EXPAND * D_MODEL
GMLP_CHUNK = 128
GMLP_GROUPS = 8
GMLP_GROUP_WIDTH = GMLP_WIDTH // GMLP_GROUPS

HEADS_PER_GROUP = D_MODEL // HEAD_DIM
DILATED_GROUPS = ((128, 1), (512, 4), (2048, 16))
N_DIL_GROUPS = len(DILATED_GROUPS)
ATTN_WIDTH = HEADS_PER_GROUP * HEAD_DIM
ATTN_BLOCK = 128

N_A_LAYERS = (DEPTH + 1) // 2
N_B_LAYERS = DEPTH // 2


def rms_norm_2(x, gain):
    xf = x.astype(jnp.float32)
    y = xf * lax.rsqrt(jnp.mean(xf * xf, axis=-1, keepdims=True) + RMS_EPS)
    return (y * gain.astype(jnp.float32)).astype(x.dtype)

def layer_norm(x, gain, bias):
    xf = x.astype(jnp.float32)
    mu = jnp.mean(xf, axis=-1, keepdims=True)
    var = jnp.mean(jnp.square(xf - mu), axis=-1, keepdims=True)
    y = (xf - mu) * lax.rsqrt(var + LN_EPS)
    return (y * gain.astype(jnp.float32) + bias.astype(jnp.float32)).astype(x.dtype)

def rope_tables(seq_len):
    inv_freq = 1.0 / (ROPE_THETA ** (jnp.arange(0, HEAD_DIM, 2, dtype=jnp.float32) / HEAD_DIM))
    ang = jnp.arange(seq_len, dtype=jnp.float32)[:, None] * inv_freq[None, :]
    return jnp.cos(ang), jnp.sin(ang)

def apply_rope(t, cos, sin):
    tf = t.astype(jnp.float32)
    t1, t2 = tf[..., : HEAD_DIM // 2], tf[..., HEAD_DIM // 2:]
    c = cos[None, :, None, :]
    s = sin[None, :, None, :]
    return jnp.concatenate([t1 * c - t2 * s, t2 * c + t1 * s], axis=-1).astype(t.dtype)

def gmlp_mixer(h, w_in, ln_g, ln_b, w_s, b_s, w_out):
    B, S, _ = h.shape
    proj = h @ w_in
    uv = jax.nn.gelu(proj[..., : 2 * GMLP_WIDTH], approximate=False)
    z = proj[..., 2 * GMLP_WIDTH:]
    u, v = uv[..., :GMLP_WIDTH], uv[..., GMLP_WIDTH:]
    v = layer_norm(v, ln_g, ln_b)
    n_chunks = S // GMLP_CHUNK
    vc = v.reshape(B, n_chunks, GMLP_CHUNK, GMLP_GROUPS, GMLP_GROUP_WIDTH)
    causal = jnp.tril(jnp.ones((GMLP_CHUNK, GMLP_CHUNK), dtype=bool))
    w_masked = jnp.where(causal[None], w_s, jnp.zeros_like(w_s))
    sv = jnp.einsum('gts,bnsgc->bntgc', w_masked, vc) + jnp.transpose(b_s)[None, None, :, :, None]
    sv = sv.reshape(B, S, GMLP_WIDTH)
    y = u * sv * jax.nn.silu(z)
    return y @ w_out

def dilated_window_attention(q, k, v, window, dilation):
    B, S, H, Dh = q.shape
    steps = window // dilation
    L = S // dilation
    Lp = ((L + ATTN_BLOCK - 1) // ATTN_BLOCK) * ATTN_BLOCK
    N = Lp // ATTN_BLOCK

    def to_blocks(t):
        t = t.reshape(B, L, dilation, H, Dh).transpose(0, 2, 1, 3, 4)
        t = jnp.pad(t, ((0, 0), (0, 0), (0, Lp - L), (0, 0), (0, 0)))
        return t.reshape(B, dilation, N, ATTN_BLOCK, H, Dh)

    qb, kb, vb = to_blocks(q), to_blocks(k), to_blocks(v)
    pad_prev = ((0, 0), (0, 0), (1, 0), (0, 0), (0, 0), (0, 0))
    kk = jnp.concatenate([jnp.pad(kb, pad_prev)[:, :, :-1], kb], axis=3)
    vv = jnp.concatenate([jnp.pad(vb, pad_prev)[:, :, :-1], vb], axis=3)

    scale = 1.0 / np.sqrt(HEAD_DIM)
    scores = jnp.einsum('brnihk,brnjhk->brnhij', qb.astype(jnp.float32), kk.astype(jnp.float32)) * scale
    i_idx = jnp.arange(ATTN_BLOCK)[:, None]
    j_idx = jnp.arange(2 * ATTN_BLOCK)[None, :]
    n_idx = jnp.arange(N)[:, None, None]
    rel = ATTN_BLOCK + i_idx - j_idx
    valid = (rel >= 0) & (rel <= steps)
    valid = valid[None] & ((n_idx - 1) * ATTN_BLOCK + j_idx[None] >= 0)
    scores = jnp.where(valid[None, None, :, None], scores, -jnp.inf)
    lse = jax.nn.logsumexp(scores, axis=-1)
    p = jnp.exp(scores - lse[..., None])
    o = jnp.einsum('brnhij,brnjhk->brnihk', p.astype(v.dtype), vv)

    o = o.reshape(B, dilation, Lp, H, Dh)[:, :, :L]
    o = o.transpose(0, 2, 1, 3, 4).reshape(B, S, H, Dh)
    lse = lse.transpose(0, 1, 2, 4, 3).reshape(B, dilation, Lp, H)[:, :, :L]
    lse = lse.transpose(0, 2, 1, 3).reshape(B, S, H)
    return o, lse

def dilated_attention_mixer(h, w_in, w_out, cos, sin):
    B, S, _ = h.shape
    proj = h @ w_in
    qkv_width = N_DIL_GROUPS * 3 * ATTN_WIDTH
    qkv = proj[..., :qkv_width].reshape(B, S, N_DIL_GROUPS, 3, HEADS_PER_GROUP, HEAD_DIM)
    z = proj[..., qkv_width:]
    outs, lses = [], []
    for g, (window, dilation) in enumerate(DILATED_GROUPS):
        q = apply_rope(qkv[:, :, g, 0], cos, sin)
        k = apply_rope(qkv[:, :, g, 1], cos, sin)
        o, lse = dilated_window_attention(q, k, qkv[:, :, g, 2], window, dilation)
        outs.append(o)
        lses.append(lse)
    alpha = jax.nn.softmax(jnp.stack(lses, axis=0), axis=0)
    o = jnp.einsum('gbsh,gbshk->bshk', alpha, jnp.stack(outs, axis=0).astype(jnp.float32))
    y = o.astype(h.dtype).reshape(B, S, ATTN_WIDTH) * jax.nn.silu(z)
    return y @ w_out

def second_inputs(seed: int = 0) -> dict:
    key = jax.random.key(seed)
    ks = jax.random.split(key, 12)
    D = D_MODEL
    x = jax.random.normal(ks[0], (BATCH, SEQ, D), jnp.float32)
    norm_pre = 1.0 + 0.05 * jax.random.normal(ks[1], (DEPTH, D), jnp.float32)
    norm_post = 1.0 + 0.05 * jax.random.normal(ks[2], (DEPTH, D), jnp.float32)
    a_w_in = jax.random.normal(ks[3], (N_A_LAYERS, D, 3 * GMLP_WIDTH), jnp.float32) * D ** -0.5
    a_ln_g = 1.0 + 0.05 * jax.random.normal(ks[4], (N_A_LAYERS, GMLP_WIDTH), jnp.float32)
    a_ln_b = 0.02 * jax.random.normal(ks[5], (N_A_LAYERS, GMLP_WIDTH), jnp.float32)
    a_w_s = jax.random.normal(ks[6], (N_A_LAYERS, GMLP_GROUPS, GMLP_CHUNK, GMLP_CHUNK), jnp.float32) * GMLP_CHUNK ** -0.5
    a_b_s = 1.0 + 0.1 * jax.random.normal(ks[7], (N_A_LAYERS, GMLP_GROUPS, GMLP_CHUNK), jnp.float32)
    a_w_out = jax.random.normal(ks[8], (N_A_LAYERS, GMLP_WIDTH, D), jnp.float32) * GMLP_WIDTH ** -0.5
    b_w_in = jax.random.normal(ks[9], (N_B_LAYERS, D, N_DIL_GROUPS * 3 * ATTN_WIDTH + ATTN_WIDTH), jnp.float32) * D ** -0.5
    b_w_out = jax.random.normal(ks[10], (N_B_LAYERS, ATTN_WIDTH, D), jnp.float32) * ATTN_WIDTH ** -0.5
    return {"x": x, "norm_pre": norm_pre, "norm_post": norm_post,
            "a_w_in": a_w_in, "a_ln_g": a_ln_g, "a_ln_b": a_ln_b, "a_w_s": a_w_s,
            "a_b_s": a_b_s, "a_w_out": a_w_out, "b_w_in": b_w_in, "b_w_out": b_w_out}

def second_block(x, norm_pre, norm_post, a_w_in, a_ln_g, a_ln_b, a_w_s, a_b_s, a_w_out, b_w_in, b_w_out):
    cos, sin = rope_tables(x.shape[1])
    for i in range(DEPTH):
        h = rms_norm_2(x, norm_pre[i])
        j = i // N_MIXERS
        if i % N_MIXERS == 0:
            y = gmlp_mixer(h, a_w_in[j], a_ln_g[j], a_ln_b[j], a_w_s[j], a_b_s[j], a_w_out[j])
        else:
            y = dilated_attention_mixer(h, b_w_in[j], b_w_out[j], cos, sin)
        x = x + rms_norm_2(y, norm_post[i])
    return x


def setup_inputs(seed=0):
    out = dict(first_inputs(seed))
    for name, value in second_inputs(seed + 1).items():
        if name != "x":
            out[name + "_2"] = value
    return out


def reference(
    x, c, ctx, c_ctx, norm_g, w_ada, b_ada, w_in, w_out, diff_q_norm, diff_k_norm, lambda_q1,
    lambda_k1, lambda_q2, lambda_k2, diff_subln, gqa_q_norm, gqa_k_norm, nat_q_norm, nat_k_norm,
    nat_rpb, norm_pre_2, norm_post_2, a_w_in_2, a_ln_g_2, a_ln_b_2, a_w_s_2, a_b_s_2, a_w_out_2,
    b_w_in_2, b_w_out_2,
):
    x = first_block(
        x, c, ctx, c_ctx, norm_g, w_ada, b_ada, w_in, w_out, diff_q_norm, diff_k_norm,
        lambda_q1, lambda_k1, lambda_q2, lambda_k2, diff_subln, gqa_q_norm, gqa_k_norm,
        nat_q_norm, nat_k_norm, nat_rpb,
    )
    return second_block(
        x, norm_pre_2, norm_post_2, a_w_in_2, a_ln_g_2, a_ln_b_2, a_w_s_2, a_b_s_2, a_w_out_2,
        b_w_in_2, b_w_out_2,
    )


_drawn_inputs = setup_inputs


def setup_inputs(seed=0):
    import zlib

    import numpy as np

    out = dict(_drawn_inputs(seed))
    spreads = {}
    factors = {'norm_g': 4.282,
     'b_ada': 4.317,
     'diff_q_norm': 8.0,
     'diff_k_norm': 8.0,
     'lambda_q1': 5.256,
     'lambda_k1': 7.892,
     'lambda_q2': 8.0,
     'lambda_k2': 8.0,
     'diff_subln': 6.096,
     'gqa_q_norm': 8.0,
     'gqa_k_norm': 8.0,
     'nat_q_norm': 8.0,
     'nat_k_norm': 8.0,
     'nat_rpb': 8.0,
     'a_ln_b_2': 30.265,
     'norm_post_2': 4.885,
     'a_ln_g_2': 8.0,
     'a_b_s_2': 4.253}
    for name, (base, spread) in spreads.items():
        noise = np.random.default_rng([zlib.crc32(name.encode()), seed]).standard_normal(out[name].shape)
        drawn = base * np.exp(spread * noise) if base else spread * noise
        out[name] = jnp.asarray(drawn.astype(out[name].dtype))
    for name, factor in factors.items():
        out[name] = (out[name] * factor).astype(out[name].dtype)
    return out
```

```python
import math
from contextlib import ExitStack

import numpy as np

import concourse.bass as bass
from concourse import mybir

F32 = mybir.dt.float32
F32R = mybir.dt.float32r
ALU = mybir.AluOpType
ACT = mybir.ActivationFunctionType
AX = mybir.AxisListType.X

P = 128
D = 1024
SEQ = 256
KT = D // P
NC = 512
HD = 64
A_HEADS, B_HEADS, B_KV, C_HEADS = 4, 6, 2, 6
EPS = 1e-6
LN_EPS = 1e-5
NEG = -1e30
GRID_W, WIN_H, WIN_W = 64, 8, 16
RPB_W = 2 * WIN_W - 1
BIAS_W = GRID_W + 2 * WIN_W
RPB_LINES = 7
GMLP = 2 * D
GROUPS = 8
DIL = 3
DIL_HEADS = D // HD
RAW = 4
SPLIT = 4
X_TILES, CTX_TILES = (0, 1), (2, 3)
ALL_TILES = X_TILES + CTX_TILES

IN1_CTX = {0: (256, 256), 1: (0, 256), 2: (256, 256), 3: (0, 256), 4: (256, 256), 5: (0, 512), 6: (0, 256)}
PROJ = {
    "in0": (7, 8), "out0": (2, 8), "in1": (7, 8), "out1": (2, 8),
    "gin": (12, 8), "gout": (2, 16), "din": (20, 8), "dout": (2, 8),
}
GIN_COLS = [4, 5, 6, 7, 0, 1, 2, 3, 8, 9, 10, 11]
BEFORE = {"out0": "in0", "in1": "out0", "out1": "in1", "gin": "out1", "gout": "gin", "din": "gout", "dout": "din"}


def tiles_of(ph):
    return ALL_TILES if ph in ("in0", "out0", "in1") else X_TILES


def columns_of(ph, c, tt):
    return IN1_CTX[c] if ph == "in1" and tt in CTX_TILES else (0, NC)


def pieces_of(ph):
    return [(ph, c, pair) for c in range(PROJ[ph][0]) for pair in range(PROJ[ph][1] // 2)]


def ada_pieces(layer):
    return [(f"ada{layer}", j, pair) for j in range(6) for pair in range(KT // 2)]


PIECES = (ada_pieces(0) + pieces_of("in0") + ada_pieces(1) + pieces_of("out0") + pieces_of("in1")
          + pieces_of("out1") + pieces_of("gin") + pieces_of("gout") + pieces_of("din") + pieces_of("dout"))
PIECE_AT = {p: n for n, p in enumerate(PIECES)}
SPLITS = [p for p in PIECES if not p[0].startswith("ada")]
SPLIT_AT = {p: n for n, p in enumerate(SPLITS)}
PROJ_BANKS = 6
PROJ_USES = [(ph, c, tt) for ph in PROJ for c in range(PROJ[ph][0]) for tt in tiles_of(ph)]
PROJ_AT = {u: n for n, u in enumerate(PROJ_USES)}

CHUNK_HEADS = {
    0: [(0, 256, 32, "A", 0), (256, 256, 32, "A", 1)],
    2: [(0, 384, 64, "B", 0), (384, 128, 64, "B", 1)],
    4: [(0, 384, 64, "C", 0), (384, 128, 64, "C", 1)],
    5: [(0, 256, 64, "C", 1)],
}
CHUNK_TILE0 = {0: 0, 2: 4, 4: 8, 5: 12}
CHUNK_VALUES = {1: (0, 256, 0), 3: (0, 128, 256), 5: (256, 256, 384), 6: (0, 128, 640)}
CHUNK_GATES = {1: (256, 256, 0), 3: (128, 384, 256), 6: (128, 384, 640)}
V_W = 768
GAIN_AT = {"A": (0, 32), "B": (64, 128), "C": (192, 256)}
SUBLN_AT = 320


def kept_columns(ph, c, tt, col, n):
    lo, w = columns_of(ph, c, tt)
    if ph == "in1" and tt in CTX_TILES:
        need = {0: (256, 512), 1: (0, 256), 2: (384, 512), 3: (0, 128), 4: (384, 512), 5: (0, 512), 6: (0, 128)}[c]
        lo, hi = need
    else:
        hi = lo + w
    a, b = max(lo, col), min(hi, col + n)
    return (a, b - a) if b > a else None


def units_of(layer):
    return [(layer, qt, kind, h) for qt in (ALL_TILES if layer == 0 else X_TILES)
            for kind, n in (("A", A_HEADS), ("B", B_HEADS), ("C", C_HEADS)) for h in range(n)]


class Count:

    def __init__(self, sem, name, known, step=1):
        self.sem, self.name, self.known, self.step, self.value, self.found = sem, name, known, step, 0, {}

    def at(self, key):
        assert key not in self.found, (self.name, key)
        self.value += self.step
        self.found[key] = self.value
        return self.sem, self.step

    def seen(self, key):
        if self.known is None:
            return self.sem, self.step
        return self.sem, self.known[self.name][key]


def first_then_second_block(nc, a, out, known):
    counts = {}
    with ExitStack() as ctx:
        def sb(name, shape, dt=F32):
            return ctx.enter_context(nc.sbuf_tensor(name, shape, dt))

        def sem(name, step=1):
            counts[name] = Count(ctx.enter_context(nc.semaphore(name)), name, known, step)
            return counts[name]

        banks = [ctx.enter_context(nc.psum_tensor(f"bank{i}", [P, 512], F32)) for i in range(8)]

        raw = sb("raw", [P, RAW, 2, NC])
        w_hi = sb("w_hi", [P, SPLIT, 2, NC], F32R)
        w_lo = sb("w_lo", [P, SPLIT, 2, NC], F32R)
        x = sb("x", [P, 4, D])
        h_hi = sb("h_hi", [P, 4096], F32R)
        h_lo = sb("h_lo", [P, 4096], F32R)
        work = sb("work", [P, 20480])
        stage = sb("stage", [P, 5120])
        ident = sb("ident", [P, P])
        gains = sb("gains", [P, 2, 384])
        base_tab = sb("base_tab", [P, 2, 2, 96])
        tabs = sb("tabs", [P, 2 * 2 * 2 * 96])
        win_mask = sb("win_mask", [P, GRID_W])
        rows = sb("rows", [56, P])
        cols = sb("cols", [P, 56])
        cvec = sb("cvec", [P, KT, 2])
        sel = sb("sel", [3, 2, P])
        ada_cols = sb("ada_cols", [P, 16, 2])
        a_scale = sb("a_scale", [P, KT, 2])
        small = sb("small", [P, 256])
        far = sb("far", [2 * C_HEADS * RPB_LINES, BIAS_W])

        def region(at, shape):
            n = int(np.prod(shape))
            v = work[:, at:at + n]
            names = " ".join("abcd"[:len(shape)])
            return v.rearrange(f"p ({names}) -> p {names}", **{k: s for k, s in zip("abcd", shape)}) if len(shape) > 1 else v

        qkT = region(0, (14, 512))
        vals = region(7168, (4, V_W))
        gate = region(10240, (4, D))
        nat_bias = region(14336, (C_HEADS, 6, GRID_W))
        ada_gate = region(16640, (3, D))
        gv = region(0, (2, GMLP))
        gu = region(4096, (2, GMLP))
        ln_gb = region(8192, (2, GMLP))
        ws_T = region(12288, (GROUPS, P))
        ws_raw = region(13312, (GROUPS, P))
        y_out = region(14336, (2, D))
        dqkT = region(0, (2 * DIL * 8, SEQ))
        dvals = region(12288, (2, DIL, D))
        dgate = region(18432, (2, D))
        post_gain = x[:, 2, :]
        dil_mask = x[:, 3, 0:768].rearrange("p (g k) -> p g k", g=DIL)

        def st(at, n):
            return stage[:, at:at + n]

        junk = st(0, 1024)
        xn = [st(1024, 1024), st(2048, 1024)]
        vt = [st(3072, 1024), st(4096, 1024)]
        sq = [st(0, 512), st(512, 512)]
        scaled = [st(1024, 512), st(1536, 512)]
        swapped = [st(2048, 512), st(2560, 512)]
        turned_in = [st(3072 + 512 * i, 512) for i in range(4)]
        probs = [st(512 * i, 512) for i in range(4)]
        pT = [st(2048 + 512 * i, 512) for i in range(3)]
        diff_o, diff_sq = st(3584, 256), st(3840, 256)
        ada_row = [st(4096, 512), st(4608, 512)]
        probs2 = [st(768 * i, 768) for i in range(3)]
        pT2 = [st(2304 + 768 * i, 768) for i in range(3)]

        SS, RS, NM, Z, RZ, NM1 = 0, 4, 8, 12, 224, 28
        DIFF_SS, DIFF_RS, LN_MV, LN_RS, POST_SS, POST_SUM, POST_RS = 40, 44, 56, 60, 64, 70, 72
        DNM, DZ, DRZ, HEAD_SS, HEAD_RS, LAM_SUM, LAM_EXP, NLAM, POWER, STATS = 80, 84, 88, 96, 128, 160, 164, 168, 170, 172

        def sm(col, n=1):
            return small[:, col:col + n]

        def ss_of(s, n):
            return sm(HEAD_SS + 16 * s, n)

        def rs_of(s, n):
            return sm(HEAD_RS + 16 * s, n)

        def tab(tt, q, which, at, d):
            at += ((tt * 2 + q) * 2 + which) * 96
            return tabs[:, at:at + d]

        landed = [sem(f"landed{i}", 16) for i in range(RAW)]
        start_loads = {n: sem(f"loaded_{n}", 16) for n in (
            "rows", "x", "ctx", "tab", "mask", "gains", "lambdas", "b_ada0", "b_ada1", "bias", "ln", "ws",
            "post", "dil_tab", "dil_mask")}
        stored = sem("stored", 16)
        bias_out = sem("bias_out", 16)
        setup_v, setup_p, setup_a, setup_t = sem("setup_v"), sem("setup_p"), sem("setup_a"), sem("setup_t")
        weights_hi, weights_lo, piece_used = sem("weights_hi"), sem("weights_lo"), sem("piece_used")
        ada_used = sem("ada_used")
        ada_row_kept, ada_post, ada_kept = sem("ada_row_kept"), sem("ada_post"), sem("ada_kept")
        ada_scale_made = sem("ada_scale_made")
        squares, rstd, normed = sem("squares"), sem("rstd"), sem("normed")
        tpose, scaled_v, scaled_a = sem("tpose"), sem("scaled_v"), sem("scaled_a")
        h_hi_made, h_lo_made = sem("h_hi_made"), sem("h_lo_made")
        projected = sem("projected")
        head_sq, head_sum, head_rstd = sem("head_sq"), sem("head_sum"), sem("head_rstd")
        head_scaled, rope_a, rope_b = sem("head_scaled"), sem("rope_a"), sem("rope_b")
        heads_made, heads_turned = sem("heads_made"), sem("heads_turned")
        values_kept = sem("values_kept")
        tabs_made = sem("tabs_made")
        out_scaled, added = sem("out_scaled"), sem("added")
        scores, row_max, exps, weighed = sem("scores"), sem("row_max"), sem("exps"), sem("weighed")
        probs_turned, pT_a, pT_v = sem("probs_turned"), sem("pT_a"), sem("pT_v")
        attended, recips, y_made = sem("attended"), sem("recips"), sem("y_made")
        diff_p, diff_v = sem("diff_p"), sem("diff_v")
        bias_masked = sem("bias_masked")
        stats, ln_v, ln_p, spatial, gated = sem("stats"), sem("ln_v"), sem("ln_p"), sem("spatial"), sem("gated")
        post_sum, post_v = sem("post_sum"), sem("post_v")
        dil_rope, dil_heads_made = sem("dil_rope"), sem("dil_heads_made")

        def made_heads(u):
            return (dil_heads_made if u[0] == "din" else heads_made).seen(u)

        def bank_of(ph, c, tt):
            return banks[PROJ_AT[(ph, c, tt)] % PROJ_BANKS]

        def freed_by(ph, c, tt):
            u = (ph, c, tt)
            if ph in ("in0", "in1"):
                return (head_scaled if c in CHUNK_HEADS else values_kept).seen(u)
            if ph in ("out0", "out1"):
                return out_scaled.seen(u)
            if ph == "gin":
                return values_kept.seen(u)
            if ph == "din":
                return (dil_rope if c < 18 and (c // 2) % 3 < 2 else values_kept).seen(u)
            return values_kept.seen(u)

        def used_last(p):
            ph, c, pair = p
            if pair == PROJ[ph][1] // 2 - 1:
                return projected.seen((ph, c, tiles_of(ph)[-1]))
            return piece_used.seen(p)

        def hT(part, ph, kt, tt):
            w = 512 if ph in ("in0", "out0", "in1", "out1") else SEQ
            return part[:, kt * w + tt * P:kt * w + (tt + 1) * P]

        def hT4(part, ph, kt0, tt):
            w = 512 if ph in ("in0", "out0", "in1", "out1") else SEQ
            return part[:, :].rearrange("p (k t) -> p k t", t=w)[:, kt0:kt0 + 4, tt * P:(tt + 1) * P]

        def last_use(ph):
            return projected.seen((ph, PROJ[ph][0] - 1, tiles_of(ph)[-1]))

        turn_uses = []

        def turn_freed(use):
            kind = use[0]
            if kind == "norm":
                _, ph, tt, half = use
                return (scaled_v if half == 0 else scaled_a).seen((ph, tt))
            if kind == "y":
                return h_lo_made.seen(use[1:])
            if kind == "heads":
                return heads_turned.seen(use[1:])
            if kind == "spatial":
                return gated.seen(use[1:])
            return setup_a.seen("ws_turned" + str(use[1]))

        def take_turn_bank(eng, use):
            turn_uses.append(use)
            n = len(turn_uses) - 1
            if n >= 2:
                eng.wait_ge(*turn_freed(turn_uses[n - 2]))
            return banks[6 + n % 2]

        def head_span(ph, c, tt):
            if ph in ("in0", "in1") and c in CHUNK_HEADS:
                parts = [kept_columns(ph, c, tt, s[0], s[1]) for s in CHUNK_HEADS[c]]
                parts = [q for q in parts if q]
                return parts[0][0], sum(q[1] for q in parts)
            if ph == "din" and c < 18 and (c // 2) % 3 < 2:
                return 0, NC
            return None

        head_chunks = {(ph, c): n for n, (ph, c) in enumerate(
            (ph, c) for ph in ("in0", "in1", "din") for c in range(PROJ[ph][0]) if head_span(ph, c, 0))}

        def turn_slot(ph, c, tt):
            return tt if ph != "din" else (head_chunks[(ph, c)] % 2) * 2 + tt

        prob_at = {}
        for layer in range(2):
            n = 0
            for u in units_of(layer):
                for m in range(2 if u[2] == "A" else 1):
                    prob_at[(u, m)] = n
                    n += 1

        def prob_slot(layer, u, m):
            return prob_at[(u, m)] % 4

        def pT_by_scalar(u, i):
            return u[2] == "A" or (u[2] == "B" and i % 2 == 0)

        def pT_seen(u, i):
            return (pT_a if pT_by_scalar(u, i) else pT_v).seen(u)

        def dil_score_place(i, g, nk):
            if nk == P:
                return banks[0], g * nk
            return (banks[1], g * nk) if g < 2 else (banks[2], 0)

        def dil_turn_bank(i, part):
            return banks[5] if part else banks[3 + i % 2]

        def rope_product(eng, to, source, off, pitch, w, d, table):
            h = d // 2
            turned = bass.AP(source, off + h, [[pitch, P], [d, w // d], [-h, 2], [1, h]])
            return eng.tensor_tensor(to.rearrange("p (n a h) -> p n a h", a=2, h=h), turned,
                                     table.rearrange("p (a h) -> p a h", a=2).unsqueeze(1).broadcast_to([P, w // d, 2, h]),
                                     ALU.mult)

        def norm_scale(ph, kt, who):
            if ph in ("in0", "in1"):
                return a_scale[:, kt, who:who + 1]
            return cols[:, (32 if ph == "gin" else 40) + kt:(33 if ph == "gin" else 41) + kt]

        def bank_of_turn(use):
            return banks[6 + turn_uses.index(use) % 2]

        def banks_of_norm(ph, tt, half):
            return bank_of_turn(("norm", ph, tt, half))

        def step_before(u, back):
            ph, c, tt = u
            if ph in ("in0", "in1"):
                order = [(ph, cc, t) for cc in range(7) for t in tiles_of(ph) if head_span(ph, cc, t)]
                i = order.index(u)
                return order[i - back] if i >= back else None
            order = [(ph, cc, t) for cc in range(20) for t in X_TILES if head_span(ph, cc, t)]
            i = order.index(u)
            return order[i - back] if i >= back else None

        def prob_reader(layer, n):
            for (u, m), k in prob_at.items():
                if u[0] == layer and k == n:
                    return u
            raise AssertionError

        def nm_col(u, m):
            return sm(NM + prob_at[(u, m)] % 4)

        def z_col(u, m):
            k = Z + 2 * (prob_at[(u, m)] % 4)
            return sm(k), sm(k + 1)

        block = ctx.enter_context(nc.Block())

        def weight_source(p):
            ph, c, pair = p
            if ph.startswith("ada"):
                src, col = a["w_ada"][int(ph[3])], c * NC
            elif ph in ("in0", "in1"):
                src, col = a["w_in"][int(ph[2])], c * NC
            elif ph in ("out0", "out1"):
                src, col = a["w_out"][int(ph[3])], c * NC
            elif ph == "gin":
                src, col = a["a_w_in_2"][0], GIN_COLS[c] * NC
            elif ph == "gout":
                src, col = a["a_w_out_2"][0], c * NC
            elif ph == "din":
                src, col = a["b_w_in_2"][0], c * NC
            else:
                src, col = a["b_w_out_2"][0], c * NC
            return src[pair * 2 * P:(pair + 1) * 2 * P, col:col + NC].rearrange("(k p) n -> p k n", p=P)

        @block.sync
        def _(sp):
            sp.dma_start(rows[0:8, :], a["c"].rearrange("b (k p) -> (b k) p", p=P)).then_inc(*start_loads["rows"].at(0))
            sp.dma_start(rows[8:16, :], a["c_ctx"].rearrange("(k p) -> k p", p=P)).then_inc(*start_loads["rows"].at(1))
            sp.dma_start(rows[16:32, :], a["norm_g"].rearrange("l (k p) -> (l k) p", p=P)).then_inc(*start_loads["rows"].at(2))
            sp.dma_start(rows[32:48, :], a["norm_pre_2"].rearrange("l (k p) -> (l k) p", p=P)).then_inc(*start_loads["rows"].at(3))
            sp.dma_start(rows[48:56, :], a["a_b_s_2"][0]).then_inc(*start_loads["rows"].at(4))
            for n, p in enumerate(PIECES):
                if p[0].startswith("ada") and p[2] == 0:
                    layer, j = int(p[0][3]), p[1]
                    g = layer * 6 + j
                    if g >= 2:
                        was = (f"ada{(g - 2) // 6}", (g - 2) % 6)
                        sp.wait_ge(*ada_post.seen(was))
                    if layer == 1 and j < 2:
                        sp.wait_ge(*tpose.seen(("heads", "in0", 5, 3)))
                    sp.dma_start(ada_row[g % 2][2:3, :], a["b_ada"][layer:layer + 1, j * NC:(j + 1) * NC]) \
                        .then_inc(*start_loads[f"b_ada{g % 2}"].at(g))
                if n >= RAW:
                    was = PIECES[n - RAW]
                    if was[0].startswith("ada"):
                        sp.wait_ge(*ada_used.seen(was))
                    else:
                        sp.wait_ge(*weights_hi.seen(was))
                        sp.wait_ge(*weights_lo.seen(was))
                sp.dma_start(raw[:, n % RAW, :, :], weight_source(p)).then_inc(*landed[n % RAW].at(p))
                if n == 4:
                    sp.dma_start(x[:, 0:2, :], a["x"][0].rearrange("(t p) d -> p t d", p=P)).then_inc(*start_loads["x"].at(0))
                    sp.dma_start(x[:, 2:4, :], a["ctx"][0].rearrange("(t p) d -> p t d", p=P)).then_inc(*start_loads["ctx"].at(0))
            o = out[0].rearrange("(t p) d -> t p d", p=P)
            for tt in X_TILES:
                sp.wait_ge(*added.seen(("dout", 1, tt)))
                sp.dma_start(o[tt], x[:, tt, :]).then_inc(*stored.at(tt))
            sp.wait_ge(*stored.seen(1))

        @block.tensor
        def _(pe):
            def arrived(eng, p):
                eng.wait_ge(*landed[PIECE_AT[p] % RAW].seen(p))

            def ada_piece(layer, j, pair):
                name = f"ada{layer}"
                p = (name, j, pair)
                arrived(pe, p)
                if pair == 0 and (layer, j) != (0, 0):
                    before = (name, j - 1) if j else (f"ada{layer - 1}", 5)
                    pe.wait_ge(*ada_kept.seen(before))
                for k in range(2):
                    kt = pair * 2 + k
                    mm = pe.matmul(banks[7][0:2, :], cvec[:, kt, :], raw[:, PIECE_AT[p] % RAW, k, :],
                                   start=(kt == 0), stop=(kt == KT - 1))
                mm.then_inc(*ada_used.at(p))

            def ada_post_step(layer, j):
                name = f"ada{layer}"
                g = layer * 6 + j
                pe.wait_ge(*ada_row_kept.seen((name, j)))
                pe.wait_ge(*start_loads[f"b_ada{g % 2}"].seen(g))
                row = ada_row[g % 2]
                if j < 4:
                    for i in range(4):
                        mm = pe.matmul(banks[7][:, 2 * i:2 * i + 2], row[0:3, i * P:(i + 1) * P], sel[0:3, :, 0],
                                       start=(i == 0), stop=(i == 3))
                    mm.then_inc(*ada_post.at((name, j)))
                else:
                    for who in range(2 if layer == 0 else 1):
                        if who == 1:
                            pe.wait_ge(*ada_kept.seen((name, j, "x")))
                        mm = pe.matmul(banks[7][:, :], sel[0:3, who, :], row[0:3, :], start=True, stop=True)
                        mm.then_inc(*ada_post.at((name, j, "x") if who == 0 and layer == 0 else (name, j)))

            def norm_turns(ph):
                for tt in tiles_of(ph):
                    pe.wait_ge(*normed.seen((ph, tt)))
                    for half in range(2):
                        bank = take_turn_bank(pe, ("norm", ph, tt, half))
                        for i in range(4):
                            kt = half * 4 + i
                            mm = pe.transpose(bank[:, i * P:(i + 1) * P], xn[tt % 2][:, kt * P:(kt + 1) * P], ident[:, :])
                        mm.then_inc(*tpose.at((ph, tt, half)))

            def y_turns(ph, src, quarters):
                for tt in tiles_of(ph):
                    for q in range(quarters):
                        bank = take_turn_bank(pe, ("y", ph, tt, q))
                        for i in range(4):
                            kt = q * 4 + i
                            mm = pe.transpose(bank[:, i * P:(i + 1) * P], src[:, tt, kt * P:(kt + 1) * P], ident[:, :])
                        mm.then_inc(*tpose.at((ph, tt, q)))

            def products(ph, c):
                kts = PROJ[ph][1]
                tts = tiles_of(ph)
                for pair in range(kts // 2):
                    p = (ph, c, pair)
                    s = SPLIT_AT[p] % SPLIT
                    pe.wait_ge(*weights_hi.seen(p))
                    pe.wait_ge(*weights_lo.seen(p))
                    for k in range(2):
                        kt = pair * 2 + k
                        for tt in tts:
                            if kt == 0:
                                n = PROJ_AT[(ph, c, tt)]
                                if n >= PROJ_BANKS:
                                    pe.wait_ge(*freed_by(*PROJ_USES[n - PROJ_BANKS]))
                            if c == 0 and kt % 4 == 0:
                                pe.wait_ge(*h_hi_made.seen((ph, tt, kt // 4)))
                                pe.wait_ge(*h_lo_made.seen((ph, tt, kt // 4)))
                            lo, w = columns_of(ph, c, tt)
                            bank = bank_of(ph, c, tt)[:, lo:lo + w]
                            first, last = kt == 0, kt == kts - 1
                            pe.matmul(bank, hT(h_lo, ph, kt, tt), w_hi[:, s, k, lo:lo + w], start=first, stop=False)
                            pe.matmul(bank, hT(h_hi, ph, kt, tt), w_lo[:, s, k, lo:lo + w], start=False, stop=False)
                            mm = pe.matmul(bank, hT(h_hi, ph, kt, tt), w_hi[:, s, k, lo:lo + w], start=False, stop=last)
                            if last:
                                mm.then_inc(*projected.at((ph, c, tt)))
                    if pair < kts // 2 - 1:
                        mm.then_inc(*piece_used.at(p))

            def head_turns(ph, c):
                for tt in tiles_of(ph):
                    span = head_span(ph, c, tt)
                    if span is None:
                        continue
                    pe.wait_ge(*made_heads((ph, c, tt)))
                    bank = take_turn_bank(pe, ("heads", ph, c, tt))
                    for i in range(span[0] // P, (span[0] + span[1]) // P):
                        mm = pe.transpose(bank[:, i * P:(i + 1) * P], turned_in[turn_slot(ph, c, tt)][:, i * P:(i + 1) * P], ident[:, :])
                    mm.then_inc(*tpose.at(("heads", ph, c, tt)))

            def project(ph, between=None):
                for c in range(PROJ[ph][0]):
                    products(ph, c)
                    if c:
                        head_turns(ph, c - 1)
                    if between:
                        between(c)
                head_turns(ph, PROJ[ph][0] - 1)

            def attention1(layer, before):
                units = units_of(layer)
                for u in PROJ_USES[PROJ_AT[(before, 6, tiles_of(before)[-1])] - 5:][:6]:
                    pe.wait_ge(*freed_by(*u))
                for use in turn_uses[-2:]:
                    pe.wait_ge(*turn_freed(use))
                todo = [lambda j=j, pair=pair: ada_piece(1, j, pair) if pair < 4 else ada_post_step(1, j)
                        for j in range(6) for pair in range(5)] if layer == 0 else []
                s_use = [0]

                def score(u):
                    _, qt, kind, h = u
                    k0 = 0 if qt in X_TILES else 256
                    for m in range(2 if kind == "A" else 1):
                        n = s_use[0]
                        s_use[0] += 1
                        if n >= 3:
                            pe.wait_ge(*exps.seen((layer, n - 3)))
                        if kind == "A":
                            col = (2 * h + m) * 32
                            tq, tk, base, d = col // P, 2 + col // P, col % P, 32
                        elif kind == "B":
                            tq, tk, base, d = 4 + h % 3, 7, (h // 3) * HD, HD
                        else:
                            tq, tk, base, d = 8 + h // 2, 11 + h // 2, (h % 2) * HD, HD
                        mm = pe.matmul(banks[n % 3][:, k0:512], qkT[base:base + d, tq, qt * P:(qt + 1) * P],
                                       qkT[base:base + d, tk, k0:512], start=True, stop=True)
                        mm.then_inc(*scores.at((u, m)))

                def turn(i):
                    u = units[i]
                    pe.wait_ge(*(weighed.seen(u) if u[2] == "A" else exps.seen((layer, prob_at[(u, 0)]))))
                    if i >= 2:
                        pe.wait_ge(*pT_seen(units[i - 2], i - 2))
                    kt0 = 0 if u[1] in X_TILES else 2
                    for j in range(kt0, 4):
                        mm = pe.transpose(banks[3 + i % 2][:, j * P:(j + 1) * P],
                                          probs[prob_slot(layer, u, 0)][:, j * P:(j + 1) * P], ident[:, :])
                    mm.then_inc(*probs_turned.at(u))

                def attend(i):
                    u = units[i]
                    _, qt, kind, h = u
                    pe.wait_ge(*pT_seen(u, i))
                    if i >= 2:
                        pe.wait_ge(*y_made.seen(units[i - 2]))
                    vcol = h * HD if kind == "A" else 256 + (h // 3) * HD if kind == "B" else 384 + h * HD
                    kt0 = 0 if qt in X_TILES else 2
                    for j in range(kt0, 4):
                        mm = pe.matmul(banks[5 + i % 2][:, 0:HD], pT[i % 3][:, j * P:(j + 1) * P],
                                       vals[:, j, vcol:vcol + HD], start=(j == kt0), stop=(j == 3))
                    mm.then_inc(*attended.at(u))

                score(units[0])
                for i in range(len(units) + 1):
                    if i + 1 < len(units):
                        score(units[i + 1])
                    if todo:
                        todo.pop(0)()
                    if i >= 1:
                        attend(i - 1)
                    if i < len(units):
                        turn(i)
                assert not todo

            def attention2():
                units = [(qt, h) for h in range(DIL_HEADS) for qt in X_TILES]
                for u in PROJ_USES[PROJ_AT[("din", 19, 1)] - 5:][:6]:
                    pe.wait_ge(*freed_by(*u))
                for use in turn_uses[-2:]:
                    pe.wait_ge(*turn_freed(use))
                pe.wait_ge(*heads_turned.seen(("din", 15, 1)))

                def score(i):
                    qt, h = units[i]
                    if i >= 2:
                        pe.wait_ge(*row_max.seen(("dil", i - 2)))
                    nk = (qt + 1) * P
                    base = (h % 2) * HD
                    for g in range(DIL):
                        bank, at = dil_score_place(i, g, nk)
                        mm = pe.matmul(bank[:, at:at + nk], dqkT[base:base + HD, g * 16 + h // 2, qt * P:(qt + 1) * P],
                                       dqkT[base:base + HD, g * 16 + 8 + h // 2, 0:nk], start=True, stop=True)
                    mm.then_inc(*scores.at(("dil", i)))

                def turn(i):
                    qt, h = units[i]
                    n = DIL * (qt + 1)
                    pe.wait_ge(*exps.seen(("dil", i)))
                    for part, lo in enumerate(range(0, n, 4)):
                        if i >= 2:
                            pe.wait_ge(*(pT_a if part else pT_v).seen(("dil", i - 2, part)))
                        for t in range(lo, min(lo + 4, n)):
                            mm = pe.transpose(dil_turn_bank(i, part)[:, (t - lo) * P:(t - lo + 1) * P],
                                              probs2[i % 3][:, t * P:(t + 1) * P], ident[:, :])
                        mm.then_inc(*probs_turned.at(("dil", i, part)))

                def attend(i):
                    qt, h = units[i]
                    pe.wait_ge(*pT_v.seen(("dil", i, 0)))
                    if qt:
                        pe.wait_ge(*pT_a.seen(("dil", i, 1)))
                    if i >= 2:
                        pe.wait_ge(*y_made.seen(("dil", i - 2)))
                    n = DIL * (qt + 1)
                    for t in range(n):
                        g, kt = t // (qt + 1), t % (qt + 1)
                        mm = pe.matmul(banks[6 + i % 2][:, 0:HD], pT2[i % 3][:, t * P:(t + 1) * P],
                                       dvals[:, kt, g, h * HD:(h + 1) * HD], start=(t == 0), stop=(t == n - 1))
                    mm.then_inc(*attended.at(("dil", i)))

                score(0)
                for i in range(len(units) + 1):
                    if i + 1 < len(units):
                        score(i + 1)
                    if i >= 1:
                        attend(i - 1)
                    if i < len(units):
                        turn(i)

            pe.wait_ge(*setup_p.seen("ident"))
            pe.wait_ge(*start_loads["rows"].seen(4))
            pe.transpose(banks[6][:, 0:56], rows[:, :], ident[0:56, 0:56]).then_inc(*setup_t.at("rows"))
            pe.wait_ge(*setup_a.seen("cvec"))
            pe.wait_ge(*setup_p.seen("sel"))
            for j in range(6):
                for pair in range(4):
                    ada_piece(0, j, pair)
                ada_post_step(0, j)
            pe.wait_ge(*setup_v.seen("cols"))
            norm_turns("in0")
            project("in0")
            attention1(0, "in0")
            pe.wait_ge(*ada_kept.seen(("ada1", 5)))
            for u in units_of(0)[-2:]:
                pe.wait_ge(*y_made.seen(u))
            y_turns("out0", gate, 2)
            project("out0")
            norm_turns("in1")
            project("in1")
            attention1(1, "in1")
            for u in units_of(1)[-2:]:
                pe.wait_ge(*y_made.seen(u))
            y_turns("out1", gate, 2)
            project("out1")
            norm_turns("gin")

            def spatial_step(c):
                if c == 0:
                    pe.wait_ge(*setup_p.seen("ws"))
                    for half in range(2):
                        bank = take_turn_bank(pe, ("ws", half))
                        for i in range(4):
                            mm = pe.transpose(bank[:, i * P:(i + 1) * P], ws_raw[:, half * 4 + i, :], ident[:, :])
                        mm.then_inc(*tpose.at(("ws", half)))
                if 5 <= c <= 8:
                    j = c - 5
                    if j == 0:
                        pe.wait_ge(*ln_p.seen(0))
                        pe.wait_ge(*ln_p.seen(1))
                        pe.wait_ge(*setup_a.seen("ws_turned1"))
                    for tt in X_TILES:
                        bank = take_turn_bank(pe, ("spatial", j, tt))
                        for i in range(2):
                            g = 2 * j + i
                            mm = pe.matmul(bank[:, i * 256:(i + 1) * 256], ws_T[:, g, :], gv[:, tt, g * 256:(g + 1) * 256],
                                           start=True, stop=True)
                        mm.then_inc(*spatial.at((j, tt)))

            project("gin", spatial_step)
            pe.wait_ge(*gated.seen(("z", 3, 1)))
            y_turns("gout", gu, 4)
            project("gout")
            norm_turns("din")
            project("din")
            attention2()
            for i in (30, 31):
                pe.wait_ge(*y_made.seen(("dil", i)))
            y_turns("dout", dgate, 2)
            project("dout")

        @block.scalar
        def _(act):
            at = [0]

            def split_until(n):
                for i in range(at[0], min(n, len(SPLITS))):
                    p = SPLITS[i]
                    act.wait_ge(*landed[PIECE_AT[p] % RAW].seen(p))
                    if i >= SPLIT:
                        act.wait_ge(*used_last(SPLITS[i - SPLIT]))
                    act.activation(w_hi[:, i % SPLIT, :, :], raw[:, PIECE_AT[p] % RAW, :, :], ACT.Copy) \
                        .then_inc(*weights_hi.at(p))
                at[0] = max(at[0], n)

            def norm(ph, bias):
                tts = tiles_of(ph)

                def square(tt):
                    if ph == "in0":
                        act.wait_ge(*start_loads["x" if tt in X_TILES else "ctx"].seen(0))
                    else:
                        act.wait_ge(*added.seen((BEFORE[ph], 1, tt)))
                    if tt:
                        act.wait_ge(*squares.seen((ph, tt - 1)))
                    elif ph == "din":
                        act.wait_ge(*values_kept.seen(("gout", 1, 1)))
                    act.activation(junk, x[:, tt, :], ACT.Square, accum_out=sm(SS + tt)) \
                        .then_inc(*squares.at((ph, tt)))

                def scale(tt):
                    act.wait_ge(*tpose.seen((ph, tt, 1)))
                    v = vt[tt % 2]
                    if tt >= 2:
                        act.wait_ge(*h_lo_made.seen((ph, tt - 2, 1)))
                    for i in range(4):
                        kt = 4 + i
                        who = 0 if tt in X_TILES else 1
                        ins = act.activation(v[:, kt * P:(kt + 1) * P], banks_of_norm(ph, tt, 1)[:, i * P:(i + 1) * P],
                                             ACT.Identity, scale=norm_scale(ph, kt, who),
                                             bias=ada_cols[:, kt, who:who + 1] if bias else 0.0)
                    ins.then_inc(*scaled_a.at((ph, tt)))
                    if tt == 0 and ph in BEFORE:
                        act.wait_ge(*last_use(BEFORE[ph]))
                    act.wait_ge(*scaled_v.seen((ph, tt)))
                    for half in range(2):
                        if half == 1:
                            act.wait_ge(*scaled_a.seen((ph, tt)))
                        act.activation(hT4(h_hi, ph, half * 4, tt), v[:, half * 512:(half + 1) * 512].rearrange("p (k t) -> p k t", k=4),
                                       ACT.Copy).then_inc(*h_hi_made.at((ph, tt, half)))

                if bias:
                    act.wait_ge(*ada_scale_made.seen(ph))
                for tt in tts:
                    square(tt)
                for tt in tts:
                    scale(tt)

            def y_parts(ph, quarters):
                first = True
                for tt in tiles_of(ph):
                    for q in range(quarters):
                        act.wait_ge(*tpose.seen((ph, tt, q)))
                        if first:
                            act.wait_ge(*last_use(BEFORE[ph]))
                            first = False
                        act.activation(hT4(h_hi, ph, q * 4, tt), bank_of_turn(("y", ph, tt, q))[:, :].rearrange("p (k t) -> p k t", k=4),
                                       ACT.Copy).then_inc(*h_hi_made.at((ph, tt, q)))

            def process_in(ph, c):
                for tt in tiles_of(ph):
                    u = (ph, c, tt)
                    bank = bank_of(*u)
                    span = head_span(*u)
                    act.wait_ge(*projected.seen(u))
                    if c in CHUNK_VALUES:
                        col, n, place = CHUNK_VALUES[c]
                        last = act.activation(vals[:, tt, place:place + n], bank[:, col:col + n], ACT.Copy)
                        if c != 5 and not kept_columns(ph, c, tt, *CHUNK_GATES[c][:2]):
                            last.then_inc(*values_kept.at(u))
                    if c in CHUNK_GATES:
                        col, n, place = CHUNK_GATES[c]
                        if kept_columns(ph, c, tt, col, n):
                            act.activation(gate[:, tt, place:place + n], bank[:, col:col + n], ACT.Silu) \
                                .then_inc(*values_kept.at(u))
                    if span:
                        s = tt % 2
                        before = step_before(u, 2)
                        if before:
                            act.wait_ge(*made_heads(before))
                        act.activation(sq[s][:, span[0]:span[0] + span[1]], bank[:, span[0]:span[0] + span[1]], ACT.Square) \
                            .then_inc(*head_sq.at(u))

            def turned_heads(ph, c):
                for tt in tiles_of(ph):
                    span = head_span(ph, c, tt)
                    if not span:
                        continue
                    act.wait_ge(*tpose.seen(("heads", ph, c, tt)))
                    t0, n = span[0] // P, span[1] // P
                    if ph == "din":
                        tile0 = (c // 6) * 16 + ((c // 2) % 3) * 8 + (c % 2) * 4
                        dst = dqkT
                    else:
                        tile0 = CHUNK_TILE0[c]
                        dst = qkT
                    act.activation(dst[:, tile0 + t0:tile0 + t0 + n, tt * P:(tt + 1) * P],
                                   bank_of_turn(("heads", ph, c, tt))[:, t0 * P:(t0 + n) * P].rearrange("p (k t) -> p k t", k=n),
                                   ACT.Copy).then_inc(*heads_turned.at((ph, c, tt)))

            def project(ph, process):
                per = PROJ[ph][1] // 2
                base = SPLIT_AT[(ph, 0, 0)]
                for c in range(PROJ[ph][0]):
                    ahead = base + (c + 1) * per + SPLIT
                    if ph in ("in0",):
                        ahead = min(ahead, base + PROJ[ph][0] * per)
                    split_until(ahead)
                    process(ph, c)
                    if c:
                        turned_heads(ph, c - 1)
                turned_heads(ph, PROJ[ph][0] - 1)

            def attention1(layer):
                units = units_of(layer)
                n_use = [0]

                def expo(u):
                    _, qt, kind, h = u
                    k0 = 0 if qt in X_TILES else 256
                    for m in range(2 if kind == "A" else 1):
                        n = n_use[0]
                        n_use[0] += 1
                        bank = banks[n % 3]
                        slot = prob_slot(layer, u, m)
                        zc = z_col(u, m)
                        act.wait_ge(*row_max.seen((u, m)))
                        if n >= 4:
                            act.wait_ge(*probs_turned.seen(prob_reader(layer, n - 4)))
                            act.wait_ge(*recips.seen(prob_reader(layer, n - 4)))
                        if kind == "C" and qt in X_TILES:
                            act.activation(probs[slot][:, 0:256], probs[slot][:, 0:256], ACT.Exp, scale=-1.0,
                                           bias=nm_col(u, m), accum_out=zc[0])
                            act.activation(probs[slot][:, 256:512], bank[:, 256:512], ACT.Exp, bias=nm_col(u, m),
                                           accum_out=zc[1]).then_inc(*exps.at((layer, n)))
                        else:
                            act.activation(probs[slot][:, k0:512], bank[:, k0:512], ACT.Exp, bias=nm_col(u, m),
                                           accum_out=zc[0]).then_inc(*exps.at((layer, n)))

                def keep_turned(i):
                    u = units[i]
                    if not pT_by_scalar(u, i):
                        return
                    k0 = 0 if u[1] in X_TILES else 256
                    act.wait_ge(*probs_turned.seen(u))
                    if i >= 3:
                        act.wait_ge(*attended.seen(units[i - 3]))
                    act.activation(pT[i % 3][:, k0:512], banks[3 + i % 2][:, k0:512], ACT.Copy).then_inc(*pT_a.at(u))

                expo(units[0])
                for i in range(len(units) + 1):
                    if i + 1 < len(units):
                        expo(units[i + 1])
                    if i < len(units):
                        keep_turned(i)
                    if len(units) - 6 <= i < len(units) - 2:
                        split_until(SPLIT_AT[(f"out{layer}", 0, 0)] + i - (len(units) - 6) + 1)

            act.wait_ge(*setup_v.seen("cols"))
            act.activation(cvec[:, :, 0], cols[:, 0:8], ACT.Silu)
            act.activation(cvec[:, :, 1], cols[:, 8:16], ACT.Silu).then_inc(*setup_a.at("cvec"))
            act.wait_ge(*setup_v.seen("lambda_sums"))
            act.activation(sm(LAM_EXP, 4), sm(LAM_SUM, 4), ACT.Exp).then_inc(*setup_a.at("lambda_exp"))
            norm("in0", True)
            split_until(4)
            project("in0", process_in)
            attention1(0)
            y_parts("out0", 2)
            project("out0", lambda ph, c: None)
            norm("in1", True)
            project("in1", process_in)
            attention1(1)
            y_parts("out1", 2)
            project("out1", lambda ph, c: None)
            norm("gin", False)

            def process_gin(ph, c):
                if c == 0:
                    for half in range(2):
                        act.wait_ge(*tpose.seen(("ws", half)))
                        act.activation(ws_T[:, half * 4:half * 4 + 4, :], bank_of_turn(("ws", half))[:, :].rearrange("p (g t) -> p g t", g=4),
                                       ACT.Copy).then_inc(*setup_a.at("ws_turned" + str(half)))
                for tt in X_TILES:
                    u = (ph, c, tt)
                    act.wait_ge(*projected.seen(u))
                    bank = bank_of(*u)
                    if c < 4:
                        act.activation(gv[:, tt, c * NC:(c + 1) * NC], bank[:, :], ACT.Gelu).then_inc(*values_kept.at(u))
                    elif c < 8:
                        act.activation(gu[:, tt, (c - 4) * NC:(c - 3) * NC], bank[:, :], ACT.Gelu).then_inc(*values_kept.at(u))
                    else:
                        j = (c - 8) * 2 + tt
                        if j >= 4:
                            act.wait_ge(*gated.seen(("z", (j - 4) // 2, (j - 4) % 2)))
                        act.activation(turned_in[j % 4], bank[:, :], ACT.Silu).then_inc(*values_kept.at(u))

            project("gin", process_gin)
            y_parts("gout", 4)

            def process_post(ph, c):
                for tt in X_TILES:
                    u = (ph, c, tt)
                    act.wait_ge(*projected.seen(u))
                    bank = bank_of(*u)
                    act.activation(y_out[:, tt, c * NC:(c + 1) * NC], bank[:, :], ACT.Copy)
                    prev = (ph, c, tt - 1) if tt else (ph, c - 1, 1)
                    if prev[1] >= 0:
                        act.wait_ge(*values_kept.seen(prev))
                    act.activation(junk[:, 0:NC], bank[:, :], ACT.Square, accum_out=sm(POST_SS + 2 * tt + c)) \
                        .then_inc(*values_kept.at(u))

            project("gout", process_post)
            norm("din", False)

            def process_din(ph, c):
                kind = (c // 2) % 3
                for tt in X_TILES:
                    u = (ph, c, tt)
                    if c >= 18:
                        act.wait_ge(*projected.seen(u))
                        act.activation(dgate[:, tt, (c - 18) * NC:(c - 17) * NC], bank_of(*u)[:, :], ACT.Silu).then_inc(*values_kept.at(u))
                    elif kind == 2:
                        act.wait_ge(*projected.seen(u))
                        act.activation(dvals[:, tt, c // 6, (c % 2) * NC:(c % 2 + 1) * NC], bank_of(*u)[:, :], ACT.Copy) \
                            .then_inc(*values_kept.at(u))

            project("din", process_din)

            for i in range(33):
                if i < 32:
                    n = DIL * P * (i % 2 + 1)
                    act.wait_ge(*row_max.seen(("dil", i)))
                    act.activation(probs2[i % 3][:, 0:n], probs2[i % 3][:, 0:n], ACT.Exp, scale=-1.0,
                                   bias=sm(DNM + i % 4), accum_out=sm(DZ + i % 4)) \
                        .then_inc(*exps.at(("dil", i)))
                j = i - 1
                if j >= 0 and j % 2 == 1:
                    act.wait_ge(*probs_turned.seen(("dil", j, 1)))
                    if j >= 3:
                        act.wait_ge(*attended.seen(("dil", j - 3)))
                    act.activation(pT2[j % 3][:, 512:768], banks[5][:, 0:256], ACT.Copy).then_inc(*pT_a.at(("dil", j, 1)))
            y_parts("dout", 2)
            project("dout", process_post)

        @block.gpsimd
        def _(pool):
            pool.memset(ident[:, :], 0.0).then_inc(*setup_p.at("zero"))
            pool.memset(sel[:, :, :], 1.0).then_inc(*setup_p.at("ones"))
            pool.wait_ge(*setup_p.seen("ones"))
            pool.affine_select(out=ident[:, :], in_=ident[:, :], compare_op=ALU.not_equal, fill=1.0, base=0,
                               pattern=[[-1, P]], channel_multiplier=1).then_inc(*setup_p.at("ident"))
            pool.affine_select(out=sel[:, :, :], in_=sel[:, :, :], compare_op=ALU.not_equal, fill=0.0, base=-1,
                               pattern=[[1, 2], [0, P]], channel_multiplier=1).then_inc(*setup_p.at("sel"))
            pool.memset(sm(POWER), -0.5).then_inc(*setup_p.at("power"))
            half = sm(POWER)
            pool.dma_start(base_tab[:, :, :, :], a["rope_1"].rearrange("(t p) a d -> p t a d", p=P)).then_inc(*start_loads["tab"].at(0))
            pool.dma_start(win_mask[:, :], a["window"]).then_inc(*start_loads["mask"].at(0))
            for layer in range(2):
                for name, col, n in (("diff_q_norm", 0, 32), ("diff_k_norm", 32, 32), ("gqa_q_norm", 64, 64),
                                     ("gqa_k_norm", 128, 64), ("nat_q_norm", 192, 64), ("nat_k_norm", 256, 64),
                                     ("diff_subln", SUBLN_AT, 64)):
                    pool.dma_start(gains[:, layer, col:col + n], a[name][layer:layer + 1, :].broadcast_to([P, n])) \
                        .then_inc(*start_loads["gains"].at((layer, name)))
            lam = st(2048, 256).rearrange("p (f l d) -> p f l d", f=4, l=2)
            for i, name in enumerate(("lambda_q1", "lambda_k1", "lambda_q2", "lambda_k2")):
                for layer in range(2):
                    pool.dma_start(lam[:, i, layer, :], a[name][layer:layer + 1, :].broadcast_to([P, 32])) \
                        .then_inc(*start_loads["lambdas"].at((i, layer)))

            def bias_in_dram():
                pool.memset(far[:, :], NEG).then_inc(*setup_p.at("far"))
                pool.wait_ge(*setup_p.seen("far"))
                lines = 2 * C_HEADS * RPB_LINES
                pool.dma_start(a["bias"], far[:, :].unsqueeze(1).broadcast_to([lines, GRID_W, BIAS_W])).then_inc(*bias_out.at("far"))
                pool.wait_ge(*bias_out.seen("far"))
                for layer in range(2):
                    for h in range(C_HEADS):
                        dst = bass.AP(a["bias"].tensor, (layer * C_HEADS + h) * RPB_LINES * GRID_W * BIAS_W + 1,
                                      [[GRID_W * BIAS_W, RPB_LINES], [BIAS_W + 1, GRID_W], [1, RPB_W]])
                        src = a["nat_rpb"][layer, h, WIN_H - 4:WIN_H + 3, :].unsqueeze(1).broadcast_to([RPB_LINES, GRID_W, RPB_W])
                        pool.dma_start(dst, src).then_inc(*bias_out.at((layer, h)))

            def bias_tiles(layer):
                pool.wait_ge(*bias_out.seen((1, C_HEADS - 1)))
                for b in range(2):
                    for h in range(C_HEADS):
                        line = (layer * C_HEADS + h) * RPB_LINES + 1 - b
                        src = a["bias"][line:line + 6, :, WIN_W:WIN_W + GRID_W].rearrange("m q k -> q m k")
                        pool.dma_start(nat_bias[b * GRID_W:(b + 1) * GRID_W, h, :, :], src) \
                            .then_inc(*start_loads["bias"].at((layer, b, h)))
                pool.wait_ge(*start_loads["bias"].seen((layer, 1, C_HEADS - 1)))
                pool.wait_ge(*start_loads["mask"].seen(0))
                for h in range(C_HEADS):
                    ins = pool.tensor_tensor(nat_bias[:, h, :, :], nat_bias[:, h, :, :],
                                             win_mask[:, :].unsqueeze(1).broadcast_to([P, 6, GRID_W]), ALU.add)
                ins.then_inc(*bias_masked.at(layer))

            def power(out_ap, in_ap, n, scale, eps, done, key):
                pool.tensor_scalar(out_ap, in_ap, scale, eps, ALU.mult, ALU.add).then_inc(*rstd.at((key, "mean")))
                pool.wait_ge(*rstd.seen((key, "mean")))
                pool.tensor_tensor(out_ap, out_ap, half.broadcast_to([P, n]), ALU.pow).then_inc(*done.at(key))

            def norm(ph):
                for tt in tiles_of(ph):
                    pool.wait_ge(*squares.seen((ph, tt)))
                    power(sm(RS + tt), sm(SS + tt), 1, 1.0 / D, EPS, rstd, (ph, tt))

            def make_tabs(layer):
                pool.wait_ge(*start_loads["tab"].seen(0))
                pool.wait_ge(*setup_v.seen("q_gains"))
                for tt in range(2):
                    for q in range(2):
                        for at, d, g in ((0, 32, 0), (32, 64, 64)):
                            g = gains[:, layer, g + q * d:g + (q + 1) * d]
                            o1 = tab(tt, q, 0, at, d)
                            o2 = tab(tt, q, 1, at, d)
                            h = d // 2
                            pool.tensor_tensor(o1, base_tab[:, tt, 0, at:at + d], g, ALU.mult)
                            pool.tensor_tensor(o2[:, 0:h], base_tab[:, tt, 1, at:at + h], g[:, h:d], ALU.mult)
                            ins = pool.tensor_tensor(o2[:, h:d], base_tab[:, tt, 1, at + h:at + d], g[:, 0:h], ALU.mult)
                ins.then_inc(*tabs_made.at(layer))

            def process_in(ph, c):
                layer = int(ph[2])
                for tt in tiles_of(ph):
                    u = (ph, c, tt)
                    span = head_span(*u)
                    if not span:
                        continue
                    d = CHUNK_HEADS[c][0][2]
                    n = span[1] // d
                    s = tt % 2
                    pool.wait_ge(*head_sum.seen(u))
                    power(rs_of(s, n), ss_of(s, n), n, 1.0 / d, EPS, head_rstd, u)
                    if c in (0, 2) and tt in X_TILES:
                        pool.wait_ge(*head_scaled.seen(u))
                        for col, w, d, name, q in CHUNK_HEADS[c]:
                            ins = rope_product(pool, swapped[s][:, col:col + w], stage, 1024 + 512 * s + col, 5120, w, d,
                                               tab(tt, q, 1, 0 if name == "A" else 32, d))
                        ins.then_inc(*rope_b.at(u))

            def attention1(layer):
                for u in units_of(layer):
                    if u[2] == "A" and u[3] == 3:
                        key = (layer, u[1])
                        pool.wait_ge(*y_made.seen(u))
                        pool.tensor_tensor(diff_sq, diff_o, diff_o, ALU.mult).then_inc(*diff_p.at((key, "sq")))
                        pool.wait_ge(*diff_v.seen((key, "sum")))
                        power(sm(DIFF_RS, 4), sm(DIFF_SS, 4), 4, 1.0 / HD, EPS, diff_p, (key, "rstd"))

            bias_in_dram()
            make_tabs(0)
            norm("in0")
            bias_tiles(0)
            for c in range(7):
                process_in("in0", c)
            attention1(0)
            norm("in1")
            pool.wait_ge(*y_made.seen(units_of(0)[-1]))
            bias_tiles(1)
            make_tabs(1)
            for c in range(7):
                process_in("in1", c)
            attention1(1)
            pool.wait_ge(*out_scaled.seen(("out1", 1, 1)))
            pool.dma_start(ws_raw[:, :, :], a["a_w_s_2"][0].rearrange("g t s -> t g s")).then_inc(*start_loads["ws"].at(0))
            pool.dma_start(ln_gb[:, 0, :], a["a_ln_g_2"].broadcast_to([P, GMLP])).then_inc(*start_loads["ln"].at(0))
            pool.dma_start(ln_gb[:, 1, :], a["a_ln_b_2"].broadcast_to([P, GMLP])).then_inc(*start_loads["ln"].at(1))
            pool.dma_start(post_gain, a["norm_post_2"][0:1, :].broadcast_to([P, D])).then_inc(*start_loads["post"].at(0))
            pool.dma_start(dil_mask, a["dil_mask"]).then_inc(*start_loads["dil_mask"].at(0))
            pool.dma_start(tabs[:, 0:512].rearrange("p (t a) -> p t a", t=2), a["rope_2"].rearrange("(t p) a -> p t a", p=P)) \
                .then_inc(*start_loads["dil_tab"].at(0))
            pool.wait_ge(*start_loads["ws"].seen(0))
            pool.affine_select(out=ws_raw[:, :, :], in_=ws_raw[:, :, :], compare_op=ALU.is_ge, fill=0.0, base=0,
                               pattern=[[0, GROUPS], [-1, P]], channel_multiplier=1).then_inc(*setup_p.at("ws"))
            norm("gin")
            for tt in X_TILES:
                pool.wait_ge(*stats.seen(("aggr", tt)))
                power(sm(LN_RS + tt), sm(LN_MV + 2 * tt + 1), 1, 1.0, LN_EPS, rstd, ("ln", tt))
                pool.wait_ge(*ln_v.seen((tt, "gain")))
                pool.tensor_tensor(gv[:, tt, :], gv[:, tt, :], ln_gb[:, 1, :], ALU.add).then_inc(*ln_p.at(tt))

            def post(ph):
                for tt in X_TILES:
                    pool.wait_ge(*values_kept.seen((ph, 1, tt)))
                    pool.tensor_tensor(sm(POST_SUM + tt), sm(POST_SS + 2 * tt), sm(POST_SS + 2 * tt + 1), ALU.add) \
                        .then_inc(*post_sum.at((ph, tt)))
                    pool.wait_ge(*post_sum.seen((ph, tt)))
                    power(sm(POST_RS + tt), sm(POST_SUM + tt), 1, 1.0 / D, EPS, rstd, (ph, tt))

            post("gout")
            norm("din")
            pool.wait_ge(*added.seen(("gout", 1, 1)))
            pool.dma_start(post_gain, a["norm_post_2"][1:2, :].broadcast_to([P, D])).then_inc(*start_loads["post"].at(1))
            for c in range(20):
                for tt in X_TILES:
                    u = ("din", c, tt)
                    if head_span(*u):
                        s = tt
                        pool.wait_ge(*dil_rope.seen(u))
                        before = step_before(u, 4)
                        if before:
                            pool.wait_ge(*tpose.seen(("heads", *before)))
                        pool.tensor_tensor(turned_in[turn_slot(*u)], sq[s], swapped[s], ALU.add).then_inc(*dil_heads_made.at(u))
            post("dout")

        @block.vector
        def _(dve):
            at = [0]

            def split_until(n):
                for i in range(at[0], min(n, len(SPLITS))):
                    p = SPLITS[i]
                    dve.wait_ge(*weights_hi.seen(p))
                    dve.tensor_tensor(w_lo[:, i % SPLIT, :, :], raw[:, PIECE_AT[p] % RAW, :, :],
                                      w_hi[:, i % SPLIT, :, :].bitcast(F32), ALU.subtract).then_inc(*weights_lo.at(p))
                at[0] = max(at[0], n)

            def ada_row_step(layer, j):
                name, g = f"ada{layer}", layer * 6 + j
                dve.wait_ge(*ada_used.seen((name, j, 3)))
                if g >= 2:
                    dve.wait_ge(*ada_post.seen((f"ada{(g - 2) // 6}", (g - 2) % 6)))
                dve.tensor_copy(ada_row[g % 2][0:2, :], banks[7][0:2, :]).then_inc(*ada_row_kept.at((name, j)))

            def ada_keep_step(layer, j):
                name = f"ada{layer}"
                if j < 4:
                    dve.wait_ge(*ada_post.seen((name, j)))
                    dve.tensor_copy(ada_cols[:, 4 * j:4 * j + 4, :], banks[7][:, 0:8].rearrange("p (k w) -> p k w", w=2)) \
                        .then_inc(*ada_kept.at((name, j)))
                    if j == 3:
                        dve.wait_ge(*ada_kept.seen((name, j)))
                        g = cols[:, 16 + 8 * layer:24 + 8 * layer].unsqueeze(2).broadcast_to([P, KT, 2])
                        dve.scalar_tensor_tensor(a_scale[:, :, :], ada_cols[:, 8:16, :], 1.0, g, ALU.add, ALU.mult) \
                            .then_inc(*ada_scale_made.at(f"in{layer}"))
                else:
                    for who in range(2 if layer == 0 else 1):
                        key = (name, j, "x") if who == 0 and layer == 0 else (name, j)
                        dve.wait_ge(*ada_post.seen(key))
                        dve.tensor_copy(ada_gate[:, 2 * layer + who, (j - 4) * NC:(j - 3) * NC], banks[7][:, :]) \
                            .then_inc(*ada_kept.at(key))

            def norm(ph, bias):
                tts = tiles_of(ph)

                def normalise(tt):
                    if tt == 0 and ph in BEFORE:
                        dve.wait_ge(*added.seen((BEFORE[ph], 1, tiles_of(BEFORE[ph])[-1])))
                    dve.wait_ge(*rstd.seen((ph, tt)))
                    if tt >= 2:
                        dve.wait_ge(*tpose.seen((ph, tt - 2, 1)))
                    dve.tensor_scalar(xn[tt % 2], x[:, tt, :], sm(RS + tt), None, ALU.mult).then_inc(*normed.at((ph, tt)))

                normalise(tts[0])
                for tt in tts:
                    if tt + 1 in tts:
                        normalise(tt + 1)
                    v = vt[tt % 2]
                    who = 0 if tt in X_TILES else 1
                    dve.wait_ge(*tpose.seen((ph, tt, 0)))
                    for i in range(4):
                        src, dst = banks_of_norm(ph, tt, 0)[:, i * P:(i + 1) * P], v[:, i * P:(i + 1) * P]
                        if bias:
                            ins = dve.tensor_scalar(dst, src, norm_scale(ph, i, who), ada_cols[:, i, who:who + 1], ALU.mult, ALU.add)
                        else:
                            ins = dve.tensor_scalar(dst, src, norm_scale(ph, i, who), None, ALU.mult)
                    ins.then_inc(*scaled_v.at((ph, tt)))
                    for half in range(2):
                        dve.wait_ge(*h_hi_made.seen((ph, tt, half)))
                        hi = hT4(h_hi, ph, half * 4, tt).bitcast(F32)
                        dve.tensor_tensor(hT4(h_lo, ph, half * 4, tt), v[:, half * 512:(half + 1) * 512].rearrange("p (k t) -> p k t", k=4),
                                          hi, ALU.subtract).then_inc(*h_lo_made.at((ph, tt, half)))

            def y_parts(ph, quarters):
                for tt in tiles_of(ph):
                    for q in range(quarters):
                        dve.wait_ge(*h_hi_made.seen((ph, tt, q)))
                        src = bank_of_turn(("y", ph, tt, q))[:, :].rearrange("p (k t) -> p k t", k=4)
                        dve.tensor_tensor(hT4(h_lo, ph, q * 4, tt), src, hT4(h_hi, ph, q * 4, tt).bitcast(F32), ALU.subtract) \
                            .then_inc(*h_lo_made.at((ph, tt, q)))

            def project(ph, process):
                per = PROJ[ph][1] // 2
                base = SPLIT_AT[(ph, 0, 0)]
                for c in range(PROJ[ph][0]):
                    ahead = base + (c + 1) * per + SPLIT
                    if ph in ("in0",):
                        ahead = min(ahead, base + PROJ[ph][0] * per)
                    split_until(ahead)
                    process(ph, c)

            def heads_in_order(t, kind, q, w):
                if kind == "B" and q == 0:
                    return t.rearrange("p (i k d) -> p k i d", k=B_KV, d=HD)
                return t

            def as_heads(t, kind, q):
                if kind == "B" and q == 0:
                    return t.rearrange("p (k i d) -> p k i d", k=B_KV, d=HD)
                return t

            def process_in(ph, c):
                layer = int(ph[2])
                if c not in CHUNK_HEADS:
                    return

                def sum_squares(tt):
                    u = (ph, c, tt)
                    lo, w = head_span(*u)
                    d = CHUNK_HEADS[c][0][2]
                    dve.wait_ge(*head_sq.seen(u))
                    dve.tensor_reduce(ss_of(tt % 2, w // d), sq[tt % 2][:, lo:lo + w].rearrange("p (n d) -> p n d", d=d), AX, ALU.add) \
                        .then_inc(*head_sum.at(u))

                def finish(tt):
                    u = (ph, c, tt)
                    s = tt % 2
                    lo, w = head_span(*u)
                    d = CHUNK_HEADS[c][0][2]
                    n = w // d
                    dve.wait_ge(*head_rstd.seen(u))
                    dve.tensor_tensor(scaled[s][:, lo:lo + w].rearrange("p (n d) -> p n d", d=d),
                                      bank_of(*u)[:, lo:lo + w].rearrange("p (n d) -> p n d", d=d),
                                      rs_of(s, n).unsqueeze(2).broadcast_to([P, n, d]), ALU.mult).then_inc(*head_scaled.at(u))
                    dve.wait_ge(*head_scaled.seen(u))
                    before = step_before(u, 4)
                    to = turned_in[turn_slot(*u)]
                    rope = c in (0, 2) and tt in X_TILES
                    parts = [(seg, kept_columns(ph, c, tt, seg[0], seg[1])) for seg in CHUNK_HEADS[c]]
                    parts = [(seg, k) for seg, k in parts if k]
                    if rope:
                        for (col, w_, d, name, q), k in parts:
                            t1 = tab(tt, q, 0, 0 if name == "A" else 32, d).unsqueeze(1).broadcast_to([P, w_ // d, d])
                            ins = dve.tensor_tensor(sq[s][:, col:col + w_].rearrange("p (n d) -> p n d", d=d),
                                                    scaled[s][:, col:col + w_].rearrange("p (n d) -> p n d", d=d), t1, ALU.mult)
                        ins.then_inc(*rope_a.at(u))
                        dve.wait_ge(*rope_a.seen(u))
                        dve.wait_ge(*rope_b.seen(u))
                    if before:
                        dve.wait_ge(*tpose.seen(("heads", *before)))
                    for (col, w_, d, name, q), k in parts:
                        dst = heads_in_order(to[:, k[0]:k[0] + k[1]], name, q, w_)
                        if rope:
                            ins = dve.tensor_tensor(dst, as_heads(sq[s][:, col:col + w_], name, q),
                                                    as_heads(swapped[s][:, col:col + w_], name, q), ALU.add)
                        else:
                            g0 = GAIN_AT[name][q]
                            g = gains[:, layer, g0:g0 + d].unsqueeze(1)
                            src = as_heads(scaled[s][:, k[0]:k[0] + k[1]], name, q)
                            if name == "B" and q == 0:
                                g = g.unsqueeze(1).broadcast_to([P, B_KV, 3, d])
                            else:
                                dst = dst.rearrange("p (n d) -> p n d", d=d)
                                src = src.rearrange("p (n d) -> p n d", d=d)
                                g = g.broadcast_to([P, k[1] // d, d])
                            ins = dve.tensor_tensor(dst, src, g, ALU.mult)
                    ins.then_inc(*heads_made.at(u))

                tts = tiles_of(ph)
                sum_squares(tts[0])
                for tt in tts:
                    if tt + 1 in tts:
                        sum_squares(tt + 1)
                    finish(tt)

            def process_out(ph, c):
                layer = int(ph[3])
                for tt in tiles_of(ph):
                    u = (ph, c, tt)
                    who = 2 if layer else 0 if tt in X_TILES else 1
                    dve.wait_ge(*projected.seen(u))
                    dve.tensor_tensor(scaled[tt % 2], bank_of(*u)[:, :], ada_gate[:, who, c * NC:(c + 1) * NC], ALU.mult) \
                        .then_inc(*out_scaled.at(u))
                    dve.wait_ge(*out_scaled.seen(u))
                    dve.tensor_tensor(x[:, tt, c * NC:(c + 1) * NC], x[:, tt, c * NC:(c + 1) * NC], scaled[tt % 2], ALU.add) \
                        .then_inc(*added.at(u))

            def attention1(layer):
                units = units_of(layer)

                def unit_max(u):
                    _, qt, kind, h = u
                    k0 = 0 if qt in X_TILES else 256
                    for m in range(2 if kind == "A" else 1):
                        n = prob_at[(u, m)]
                        bank = banks[n % 3]
                        dve.wait_ge(*scores.seen((u, m)))
                        if kind == "C" and qt in X_TILES:
                            dve.tensor_reduce(sm(NM1 + n % 4), bank[:, 256:512], AX, ALU.max, negate=True).then_inc(*row_max.at((u, "ctx")))
                            dve.wait_ge(*row_max.seen((u, "ctx")))
                            dve.wait_ge(*bias_masked.seen(layer))
                            if n >= 4:
                                dve.wait_ge(*probs_turned.seen(prob_reader(layer, n - 4)))
                            near = nat_bias[:, h, 2 - 2 * qt:6 - 2 * qt, :].rearrange("p m k -> p (m k)")
                            dve.tensor_tensor_reduce(probs[n % 4][:, 0:256], bank[:, 0:256], near, -1.0, sm(NM1 + n % 4),
                                                     ALU.add, ALU.min, nm_col(u, m)).then_inc(*row_max.at((u, m)))
                        else:
                            dve.tensor_reduce(nm_col(u, m), bank[:, k0:512], AX, ALU.max, negate=True).then_inc(*row_max.at((u, m)))

                def weigh(i):
                    u = units[i]
                    _, qt, kind, h = u
                    k0 = 0 if qt in X_TILES else 256
                    n = prob_at[(u, 0)]
                    rz = sm(RZ + n % 8)
                    if kind == "A":
                        rz1 = sm(RZ + (n + 1) % 8)
                        dve.wait_ge(*exps.seen((layer, n + 1)))
                        dve.reciprocal(rz, z_col(u, 0)[0])
                        dve.reciprocal(rz1, z_col(u, 1)[0]).then_inc(*recips.at(u))
                        dve.wait_ge(*recips.seen(u))
                        p0, p1 = probs[n % 4][:, k0:512], probs[(n + 1) % 4][:, k0:512]
                        dve.tensor_scalar(p0, p0, rz, None, ALU.mult).then_inc(*weighed.at((u, 0)))
                        dve.tensor_scalar(sm(NM1 + 4), rz1, sm(NLAM + layer), None, ALU.mult).then_inc(*weighed.at((u, 1)))
                        dve.wait_ge(*weighed.seen((u, 1)))
                        dve.scalar_tensor_tensor(p0, p1, sm(NM1 + 4), p0, ALU.mult, ALU.add).then_inc(*weighed.at(u))
                    elif kind == "C" and qt in X_TILES:
                        dve.wait_ge(*exps.seen((layer, n)))
                        dve.tensor_tensor(z_col(u, 0)[0], z_col(u, 0)[0], z_col(u, 0)[1], ALU.add).then_inc(*weighed.at((u, 0)))
                        dve.wait_ge(*weighed.seen((u, 0)))
                        dve.reciprocal(rz, z_col(u, 0)[0]).then_inc(*recips.at(u))
                    else:
                        dve.wait_ge(*exps.seen((layer, n)))
                        dve.reciprocal(rz, z_col(u, 0)[0]).then_inc(*recips.at(u))

                def keep_turned(i):
                    u = units[i]
                    if pT_by_scalar(u, i):
                        return
                    k0 = 0 if u[1] in X_TILES else 256
                    dve.wait_ge(*probs_turned.seen(u))
                    if i >= 3:
                        dve.wait_ge(*attended.seen(units[i - 3]))
                    dve.tensor_copy(pT[i % 3][:, k0:512], banks[3 + i % 2][:, k0:512]).then_inc(*pT_v.at(u))

                def output(i):
                    u = units[i]
                    _, qt, kind, h = u
                    key = (layer, qt)
                    o = banks[5 + i % 2][:, 0:HD]
                    dve.wait_ge(*attended.seen(u))
                    if kind == "A":
                        dve.tensor_copy(diff_o[:, h * HD:(h + 1) * HD], o).then_inc(*y_made.at(u))
                        return
                    col = (256 if kind == "B" else 640) + h * HD
                    g = gate[:, qt, col:col + HD]
                    dve.scalar_tensor_tensor(g, o, sm(RZ + prob_at[(u, 0)] % 8), g, ALU.mult, ALU.mult).then_inc(*y_made.at(u))
                    if kind == "B" and h == 1:
                        dve.wait_ge(*diff_p.seen((key, "sq")))
                        dve.tensor_reduce(sm(DIFF_SS, 4), diff_sq.rearrange("p (h d) -> p h d", d=HD), AX, ALU.add) \
                            .then_inc(*diff_v.at((key, "sum")))
                    if kind == "B" and h == 3:
                        o4 = diff_o.rearrange("p (h d) -> p h d", d=HD)
                        g4 = gate[:, qt, 0:256].rearrange("p (h d) -> p h d", d=HD)
                        sub = gains[:, layer, SUBLN_AT:SUBLN_AT + HD].unsqueeze(1).broadcast_to([P, A_HEADS, HD])
                        dve.wait_ge(*diff_p.seen((key, "rstd")))
                        dve.tensor_tensor(g4, g4, sub, ALU.mult).then_inc(*diff_v.at((key, "gates")))
                        dve.tensor_tensor(o4, o4, sm(DIFF_RS, 4).unsqueeze(2).broadcast_to([P, A_HEADS, HD]), ALU.mult) \
                            .then_inc(*diff_v.at((key, "scaled")))
                        dve.wait_ge(*diff_v.seen((key, "scaled")))
                        dve.tensor_tensor(g4, g4, o4, ALU.mult).then_inc(*diff_v.at((key, "done")))

                unit_max(units[0])
                for i in range(len(units) + 1):
                    if i < len(units):
                        weigh(i)
                    if i + 1 < len(units):
                        unit_max(units[i + 1])
                    if layer == 0 and i < 30:
                        if i % 5 == 3:
                            ada_row_step(1, i // 5)
                        if i % 5 == 4:
                            ada_keep_step(1, i // 5)
                    if i >= 1:
                        output(i - 1)
                    if i < len(units):
                        keep_turned(i)
                    if len(units) - 6 <= i < len(units) - 2:
                        split_until(SPLIT_AT[(f"out{layer}", 0, 0)] + i - (len(units) - 6) + 1)

            dve.wait_ge(*setup_t.seen("rows"))
            dve.tensor_copy(cols[:, :], banks[6][:, 0:56]).then_inc(*setup_v.at("cols"))
            dve.wait_ge(*start_loads["lambdas"].seen((3, 1)))
            lam = st(2048, 256).rearrange("p (f l d) -> p f l d", f=4, l=2)
            for layer in range(2):
                for i in range(2):
                    ins = dve.tensor_tensor_reduce(st(2304 + 32 * (2 * layer + i), 32), lam[:, 2 * i, layer, :], lam[:, 2 * i + 1, layer, :],
                                                   1.0, 0.0, ALU.mult, ALU.add, sm(LAM_SUM + 2 * layer + i))
            ins.then_inc(*setup_v.at("lambda_sums"))
            dve.wait_ge(*start_loads["gains"].seen((1, "diff_subln")))
            for layer in range(2):
                lam_init = 0.8 - 0.6 * math.exp(-0.3 * layer)
                for col, n, f in ((0, 32, 32 ** -0.5), (64, 64, HD ** -0.5), (192, 64, HD ** -0.5), (SUBLN_AT, 64, 1 - lam_init)):
                    g = gains[:, layer, col:col + n]
                    ins = dve.tensor_scalar(g, g, f, None, ALU.mult)
            ins.then_inc(*setup_v.at("q_gains"))
            dve.wait_ge(*setup_a.seen("lambda_exp"))
            for layer in range(2):
                lam_init = 0.8 - 0.6 * math.exp(-0.3 * layer)
                e1, e2 = sm(LAM_EXP + 2 * layer), sm(LAM_EXP + 2 * layer + 1)
                dve.tensor_tensor(sm(NLAM + layer), e2, e1, ALU.subtract).then_inc(*setup_v.at(("lam", layer)))
                dve.wait_ge(*setup_v.seen(("lam", layer)))
                dve.tensor_scalar(sm(NLAM + layer), sm(NLAM + layer), -lam_init, None, ALU.add).then_inc(*setup_v.at(("nlam", layer)))
            for j in range(6):
                ada_row_step(0, j)
                ada_keep_step(0, j)
            norm("in0", True)
            split_until(4)
            dve.wait_ge(*tabs_made.seen(0))
            project("in0", process_in)
            attention1(0)
            y_parts("out0", 2)
            project("out0", process_out)
            norm("in1", True)
            dve.wait_ge(*tabs_made.seen(1))
            project("in1", process_in)
            attention1(1)
            y_parts("out1", 2)
            project("out1", process_out)
            norm("gin", False)

            def process_gin(ph, c):
                if c < 4:
                    for tt in X_TILES:
                        dve.wait_ge(*values_kept.seen((ph, c, tt)))
                        dve.bn_stats(sm(STATS + 24 * tt + 6 * c, 6), gv[:, tt, c * NC:(c + 1) * NC]).then_inc(*stats.at((c, tt)))
                if c == 3:
                    for tt in X_TILES:
                        dve.wait_ge(*stats.seen((c, tt)))
                        dve.bn_aggr(sm(LN_MV + 2 * tt, 2), sm(STATS + 24 * tt, 24)).then_inc(*stats.at(("aggr", tt)))
                    dve.wait_ge(*start_loads["ln"].seen(1))
                    for tt in X_TILES:
                        dve.wait_ge(*rstd.seen(("ln", tt)))
                        dve.tensor_scalar(gv[:, tt, :], gv[:, tt, :], sm(LN_MV + 2 * tt), sm(LN_RS + tt), ALU.subtract, ALU.mult) \
                            .then_inc(*ln_v.at((tt, "scaled")))
                        dve.wait_ge(*ln_v.seen((tt, "scaled")))
                        dve.tensor_tensor(gv[:, tt, :], gv[:, tt, :], ln_gb[:, 0, :], ALU.mult).then_inc(*ln_v.at((tt, "gain")))
                if 5 <= c <= 8:
                    j = c - 5
                    for tt in X_TILES:
                        dve.wait_ge(*spatial.seen((j, tt)))
                        for i in range(2):
                            g = 2 * j + i
                            bank = bank_of_turn(("spatial", j, tt))
                            u = gu[:, tt, g * 256:(g + 1) * 256]
                            ins = dve.scalar_tensor_tensor(u, bank[:, i * 256:(i + 1) * 256], cols[:, 48 + g:49 + g], u, ALU.add, ALU.mult)
                        ins.then_inc(*gated.at((j, tt)))
                if c >= 8:
                    for tt in X_TILES:
                        dve.wait_ge(*values_kept.seen((ph, c, tt)))
                        u = gu[:, tt, (c - 8) * NC:(c - 7) * NC]
                        dve.tensor_tensor(u, u, turned_in[((c - 8) * 2 + tt) % 4], ALU.mult).then_inc(*gated.at(("z", c - 8, tt)))

            project("gin", process_gin)
            y_parts("gout", 4)

            def process_post(ph, c):
                if c == 0:
                    return
                dve.wait_ge(*start_loads["post"].seen(0 if ph == "gout" else 1))
                for tt in X_TILES:
                    dve.wait_ge(*rstd.seen((ph, tt)))
                    dve.scalar_tensor_tensor(y_out[:, tt, :], y_out[:, tt, :], sm(POST_RS + tt), post_gain, ALU.mult, ALU.mult) \
                        .then_inc(*post_v.at((ph, tt)))
                    dve.wait_ge(*post_v.seen((ph, tt)))
                    dve.tensor_tensor(x[:, tt, :], x[:, tt, :], y_out[:, tt, :], ALU.add).then_inc(*added.at((ph, 1, tt)))

            project("gout", process_post)
            norm("din", False)
            dve.wait_ge(*start_loads["dil_tab"].seen(0))
            dve.wait_ge(*start_loads["dil_mask"].seen(0))

            def process_din(ph, c):
                for tt in X_TILES:
                    u = (ph, c, tt)
                    if not head_span(*u):
                        continue
                    q = (c // 2) % 3
                    dve.wait_ge(*projected.seen(u))
                    before = step_before(u, 2)
                    if before:
                        dve.wait_ge(*made_heads(before))
                    t = tt * 256 + q * 128
                    dve.tensor_tensor(sq[tt].rearrange("p (n d) -> p n d", d=HD), bank_of(*u)[:, :].rearrange("p (n d) -> p n d", d=HD),
                                      tabs[:, t:t + HD].unsqueeze(1).broadcast_to([P, 8, HD]), ALU.mult)
                    rope_product(dve, swapped[tt], bank_of(*u), 0, 512, NC, HD, tabs[:, t + HD:t + 2 * HD]).then_inc(*dil_rope.at(u))

            project("din", process_din)

            def dil_max(i):
                qt = i % 2
                nk = (qt + 1) * P
                dve.wait_ge(*scores.seen(("dil", i)))
                if i >= 3:
                    dve.wait_ge(*probs_turned.seen(("dil", i - 3, (i - 3) % 2)))
                mask = dil_mask[:, :, 2 * P - nk:2 * P]
                to = probs2[i % 3]
                if qt == 0:
                    dve.tensor_tensor_reduce(to[:, 0:384].rearrange("p (g k) -> p g k", g=3), banks[0][:, 0:384].rearrange("p (g k) -> p g k", g=3),
                                             mask, -1.0, -NEG, ALU.add, ALU.min, sm(DNM + i % 4)).then_inc(*row_max.at(("dil", i)))
                else:
                    dve.tensor_tensor_reduce(to[:, 0:512].rearrange("p (g k) -> p g k", g=2), banks[1][:, 0:512].rearrange("p (g k) -> p g k", g=2),
                                             mask[:, 0:2, :], -1.0, -NEG, ALU.add, ALU.min, sm(NM1)).then_inc(*row_max.at(("dil", i, 0)))
                    dve.wait_ge(*row_max.seen(("dil", i, 0)))
                    dve.tensor_tensor_reduce(to[:, 512:768], banks[2][:, 0:256], mask[:, 2, :], -1.0, sm(NM1), ALU.add, ALU.min,
                                             sm(DNM + i % 4)).then_inc(*row_max.at(("dil", i)))

            dil_max(0)
            for i in range(33):
                if i < 31:
                    dil_max(i + 1)
                j = i - 1
                if j >= 0:
                    qt, h = j % 2, j // 2
                    dve.wait_ge(*exps.seen(("dil", j)))
                    dve.reciprocal(sm(DRZ + j % 4), sm(DZ + j % 4)).then_inc(*recips.at(("dil", j)))
                    dve.wait_ge(*recips.seen(("dil", j)))
                    dve.wait_ge(*attended.seen(("dil", j)))
                    g = dgate[:, qt, h * HD:(h + 1) * HD]
                    dve.scalar_tensor_tensor(g, banks[6 + j % 2][:, 0:HD], sm(DRZ + j % 4), g, ALU.mult, ALU.mult) \
                        .then_inc(*y_made.at(("dil", j)))
                if i < 32:
                    n = 384 if i % 2 == 0 else 512
                    dve.wait_ge(*probs_turned.seen(("dil", i, 0)))
                    if i >= 3:
                        dve.wait_ge(*attended.seen(("dil", i - 3)))
                    dve.tensor_copy(pT2[i % 3][:, 0:n], dil_turn_bank(i, 0)[:, 0:n]).then_inc(*pT_v.at(("dil", i, 0)))
            y_parts("dout", 2)
            project("dout", process_post)

    return {name: c.found for name, c in counts.items()}


_INS = ['x', 'c', 'ctx', 'c_ctx', 'norm_g', 'w_ada', 'b_ada', 'w_in', 'w_out', 'diff_q_norm', 'diff_k_norm',
        'lambda_q1', 'lambda_k1', 'lambda_q2', 'lambda_k2', 'diff_subln', 'gqa_q_norm', 'gqa_k_norm', 'nat_q_norm',
        'nat_k_norm', 'nat_rpb', 'norm_pre_2', 'norm_post_2', 'a_w_in_2', 'a_ln_g_2', 'a_ln_b_2', 'a_w_s_2',
        'a_b_s_2', 'a_w_out_2', 'b_w_in_2', 'b_w_out_2']


def _constants():
    t = np.arange(SEQ)
    row, col = (t // GRID_W).astype(np.float32), (t % GRID_W).astype(np.float32)
    parts = []
    for d in (32, HD):
        nf = d // 4
        inv = (np.float32(10000.0) ** (-np.arange(nf, dtype=np.float32) / np.float32(nf))).astype(np.float32)
        ang = np.concatenate([row[:, None] * inv, col[:, None] * inv], axis=-1)
        c, s = np.cos(ang), np.sin(ang)
        parts.append((np.concatenate([c, c], 1), np.concatenate([-s, s], 1)))
    rope_1 = np.stack([np.concatenate([p[i] for p in parts], 1) for i in range(2)], 1).astype(np.float32)
    inv = (1.0 / (np.float32(10000.0) ** (np.arange(0, HD, 2, dtype=np.float32) / np.float32(HD)))).astype(np.float32)
    ang = t.astype(np.float32)[:, None] * inv[None, :]
    c, s = np.cos(ang), np.sin(ang)
    c2, s2 = np.concatenate([c, c], 1), np.concatenate([-s, s], 1)
    f = HD ** -0.5
    rope_2 = np.concatenate([c2 * f, s2 * f, c2, s2], 1).astype(np.float32)
    q = (np.arange(P) % GRID_W)[:, None]
    k = np.arange(GRID_W)[None, :]
    first = np.clip(q - WIN_W // 2, 0, GRID_W - WIN_W)
    window = np.where((k >= first) & (k < first + WIN_W), 0.0, NEG).astype(np.float32)
    rel = P + np.arange(P)[:, None] - np.arange(SEQ)[None, :]
    dil = [np.where((rel >= 0) & (rel % r == 0) & (rel <= w), 0.0, NEG) for w, r in ((128, 1), (512, 4), (2048, 16))]
    return {"rope_1": rope_1, "rope_2": rope_2, "window": window, "dil_mask": np.stack(dil, 1).astype(np.float32)}


def kernel(**inputs):
    import concourse.bacc as _bacc
    from concourse.bass_utils import run_bass_kernel_spmd as _run

    arrays = {f"in_{n}_dram": np.ascontiguousarray(inputs[n]) for n in _INS}
    arrays.update({f"in_{n}_dram": v for n, v in _constants().items()})

    def build(known):
        nc = _bacc.Bacc("TRN2", target_bir_lowering=False, num_devices=1)
        a = {n[3:-5]: nc.dram_tensor(n, v.shape, F32, kind="ExternalInput").ap() for n, v in arrays.items()}
        a["bias"] = nc.dram_tensor("bias", (2 * C_HEADS * RPB_LINES, GRID_W, BIAS_W), F32).ap()
        out = nc.dram_tensor("out_0_dram", (1, SEQ, D), F32, kind="ExternalOutput").ap()
        return nc, first_then_second_block(nc, a, out, known)

    _, known = build(None)
    nc, _ = build(known)
    r = _run(nc, [arrays], core_ids=[0])
    return r.results[0]["out_0_dram"]
```

```python
import math
from contextlib import ExitStack

import numpy as np

import concourse.bass as bass
from concourse import mybir

F32 = mybir.dt.float32
F32R = mybir.dt.float32r
ALU = mybir.AluOpType
ACT = mybir.ActivationFunctionType
AX = mybir.AxisListType.X

P = 128
D = 1024
SEQ = 256
KT = D // P
NC = 512
HD = 64
A_HEADS, B_HEADS, B_KV, C_HEADS = 4, 6, 2, 6
EPS = 1e-6
LN_EPS = 1e-5
NEG = -1e30
GRID_W, WIN_H, WIN_W = 64, 8, 16
RPB_W = 2 * WIN_W - 1
BIAS_W = GRID_W + 2 * WIN_W
ROWS = 56 + 2 * 24
STAGE_W = 6144
RPB_LINES = 7
GMLP = 2 * D
GROUPS = 8
DIL = 3
DIL_HEADS = D // HD
X_TILES, CTX_TILES = (0, 1), (2, 3)
ALL_TILES = X_TILES + CTX_TILES

IN1_CTX = {0: (256, 256), 1: (0, 256), 2: (256, 256), 3: (0, 256), 4: (256, 256), 5: (0, 512), 6: (0, 256)}
PROJ = {
    "in0": (7, 8), "out0": (2, 8), "in1": (7, 8), "out1": (2, 8),
    "gin": (12, 8), "gout": (2, 16), "din": (20, 8), "dout": (2, 8),
}
DIN_COLS = [2 * i for i in range(9)] + [18, 19] + [2 * i + 1 for i in range(9)]
GIN_COLS = [4, 5, 6, 7, 0, 1, 2, 3, 8, 9, 10, 11]
FOLLOWING = {"out0": "in1", "out1": "gin", "gout": "din", "dout": None}
TURNED_AFTER = {(2, 0): 0, (2, 1): 1, (3, 0): 2, (3, 1): 3}


def tiles_of(ph):
    return ALL_TILES if ph in ("in0", "out0", "in1") else X_TILES


def columns_of(ph, c, tt):
    return IN1_CTX[c] if ph == "in1" and tt in CTX_TILES else (0, NC)


def pieces_of(ph):
    return [(ph, c, pair) for c in range(PROJ[ph][0]) for pair in range(PROJ[ph][1] // 2)]


def ada_pieces(layer, chunks):
    return [(f"ada{layer}", j, pair) for j in chunks for pair in range(KT // 2)]


RAW = 3
SPLIT = 4
ADA_BESIDE = dict(zip(pieces_of("in0")[4:], ada_pieces(0, (4, 5)) + ada_pieces(1, range(4))))
ADA_READY = {p: was[:2] for p, was in zip(pieces_of("in0")[5:], ADA_BESIDE.values()) if was[2] == 3}


def first_pieces():
    ahead = pieces_of("in0") + [None] * SPLIT
    order = ahead[:2 * SPLIT]
    for n, p in enumerate(pieces_of("in0")[SPLIT:], SPLIT):
        order += [ahead[n + SPLIT], ADA_BESIDE[p]]
    return [p for p in order if p]


PIECES = (ada_pieces(0, range(4)) + first_pieces() + ada_pieces(1, (4, 5)) + pieces_of("out0") + pieces_of("in1")
          + pieces_of("out1") + pieces_of("gin") + pieces_of("gout") + pieces_of("din") + pieces_of("dout"))
PIECE_AT = {p: n for n, p in enumerate(PIECES)}
SPLITS = [p for p in PIECES if not p[0].startswith("ada")]
SPLIT_AT = {p: n for n, p in enumerate(SPLITS)}
BESIDE = ("in0", "in1", "din")
SCORE_BANKS, TURN_BANK, OUT_BANK = (4, 5), 6, 7
FIRST_BESIDE = {"in0": (2, 1), "in1": (2, 1), "din": (11, 1)}

CHUNK_HEADS = {
    0: [(0, 256, 32, "A", 0), (256, 256, 32, "A", 1)],
    2: [(0, 384, 64, "B", 0), (384, 128, 64, "B", 1)],
    4: [(0, 384, 64, "C", 0), (384, 128, 64, "C", 1)],
    5: [(0, 256, 64, "C", 1)],
}
CHUNK_TILE0 = {0: 0, 2: 4, 4: 8, 5: 12}
CHUNK_VALUES = {1: (0, 256, 0), 3: (0, 128, 256), 5: (256, 256, 384), 6: (0, 128, 640)}
CHUNK_GATES = {1: (256, 256, 0), 3: (128, 384, 256), 6: (128, 384, 640)}
V_W = 768
GAIN_AT = {"A": (0, 32), "B": (64, 128), "C": (192, 256)}
SUBLN_AT = 320


def kept_columns(ph, c, tt, col, n):
    lo, w = columns_of(ph, c, tt)
    if ph == "in1" and tt in CTX_TILES:
        need = {0: (256, 512), 1: (0, 256), 2: (384, 512), 3: (0, 128), 4: (384, 512), 5: (0, 512), 6: (0, 128)}[c]
        lo, hi = need
    else:
        hi = lo + w
    a, b = max(lo, col), min(hi, col + n)
    return (a, b - a) if b > a else None


def units_of(layer):
    return [(layer, qt, kind, h) for kind, n in (("A", A_HEADS), ("B", B_HEADS), ("C", C_HEADS))
            for qt in (ALL_TILES if layer == 0 else X_TILES) for h in range(n)]


def steps_beside(ph):
    c0, pair0 = FIRST_BESIDE[ph]
    slots = [p for p in pieces_of(ph) if (p[1], p[2]) >= (c0, pair0)]
    if ph == "din":
        slots = slots[::2][:DIL_HEADS - 1]
    return {(p, 1): i for i, p in enumerate(slots)}


def fill_of(layer):
    first = len(steps_beside(f"in{layer}"))
    tasks = {}
    if layer == 0:
        tasks = {first + i + i // 4: [("products", p)] for i, p in enumerate(ada_pieces(1, (4, 5)))}
        for i, j in ((0, 3), (5, 4), (10, 5)):
            tasks.setdefault(first + i, []).append(("ada", "ada1", j))
    first = 44 if layer == 0 else 23
    tts = ALL_TILES if layer == 0 else X_TILES
    for i, tt in enumerate(tts):
        tasks.setdefault(first + i, []).append(("y", tt))
    for i in range(SPLIT):
        tasks.setdefault(len(units_of(layer)) - SPLIT + i, []).append(("split", i))
    return tasks


class Count:

    def __init__(self, sem, name, known, step=1):
        self.sem, self.name, self.known, self.step, self.value, self.found = sem, name, known, step, 0, {}

    def at(self, key):
        assert key not in self.found, (self.name, key)
        self.value += self.step
        self.found[key] = self.value
        return self.sem, self.step

    def seen(self, key):
        if self.known is None:
            return self.sem, self.step
        return self.sem, self.known[self.name][key]


def first_then_second_block(nc, a, out, known):
    counts = {}
    with ExitStack() as ctx:
        def sb(name, shape, dt=F32):
            return ctx.enter_context(nc.sbuf_tensor(name, shape, dt))

        def sem(name, step=1):
            counts[name] = Count(ctx.enter_context(nc.semaphore(name)), name, known, step)
            return counts[name]

        banks = [ctx.enter_context(nc.psum_tensor(f"bank{i}", [P, 512], F32)) for i in range(8)]

        raw = sb("raw", [P, RAW, 2, NC])
        w_hi = sb("w_hi", [P, SPLIT, 2, NC], F32R)
        w_lo = sb("w_lo", [P, SPLIT, 2, NC], F32R)
        x = sb("x", [P, 4, D])
        h_hi = sb("h_hi", [P, 4096], F32R)
        h_lo = sb("h_lo", [P, 4096], F32R)
        work = sb("work", [P, 20736])
        stage = sb("stage", [P, STAGE_W])
        ident = sb("ident", [P, P])
        gains = sb("gains", [P, 2, 384])
        base_tab = sb("base_tab", [P, 2, 3, 48])
        tabs = sb("tabs", [P, 2 * 2 * 2 * 96])
        win_mask = sb("win_mask", [P, GRID_W])
        cols = sb("cols", [P, ROWS])
        cvec = sb("cvec", [P, KT, 2])
        ones = sb("ones", [P, P])
        ada_cols = sb("ada_cols", [P, 16, 2])
        a_scale = sb("a_scale", [P, KT, 2])
        small = sb("small", [P, 240])

        def region(at, shape):
            n = int(np.prod(shape))
            v = work[:, at:at + n]
            names = " ".join("abcd"[:len(shape)])
            return v.rearrange(f"p ({names}) -> p {names}", **{k: s for k, s in zip("abcd", shape)}) if len(shape) > 1 else v

        qkT = region(0, (14, 512))
        vals = region(7168, (4, V_W))
        gate = region(10240, (4, D))
        nat_bias = region(14336, (C_HEADS, 6, GRID_W))
        ada_gate = region(16640, (3, D))
        ada_sums = [region(1024 * i, (2, NC)) for i in range(2)] + [region(19712, (2, NC))]
        gv = region(0, (2, GMLP))
        gu = region(4096, (2, GMLP))
        ln_gb = region(8192, (2, GMLP))
        ws_T = region(12288, (GROUPS, P))
        ws_raw = region(13312, (GROUPS, P))
        y_out = region(14336, (2, D))
        dqkT = region(0, (2 * DIL * 8, SEQ))
        dvals = region(12288, (2, DIL, D))
        dgate = region(18432, (2, D))
        post_gain = x[:, 2, :]
        dil_mask = x[:, 3, 0:768].rearrange("p (g k) -> p g k", g=DIL)

        def st(at, n):
            return stage[:, at:at + n]

        heads = [st(512 * i, 512) for i in range(4)]
        swapped = [st(2048, 512), st(2560, 512)]
        sq = st(2560, 512)
        probs = [st(3072 + 512 * i, 512) for i in range(4)]
        pT = [st(5120 + 512 * i, 512) for i in range(2)]
        probs2 = [st(3072, 768), st(3840, 768), gains[:, :, :].rearrange("p l c -> p (l c)")]
        pT2 = [st(4608 + 768 * i, 768) for i in range(2)]
        xn = [st(1024 * i, 1024) for i in range(2)]
        vt = [st(2048 + 1024 * i, 1024) for i in range(2)]
        junk = st(4096, 512)
        silu_z = [st(2048 + 512 * i, 512) for i in range(4)]
        out_part = [st(5120, 512), st(5632, 512)]
        rows = stage[0:ROWS, 4608:4608 + P]
        far = stage[0:2 * C_HEADS * RPB_LINES, 4736:4736 + BIAS_W]
        lam = st(4832, 256).rearrange("p (f l d) -> p f l d", f=4, l=2)

        SS, RS, NM, Z, RZ, NM1 = 0, 8, 12, 16, 224, 24
        DIFF_SS, DIFF_RS, LN_MV, LN_RS, POST_SS, POST_SUM, POST_RS = 32, 48, 64, 68, 70, 74, 76
        DNM, DZ, DRZ, HEAD_SS, HEAD_RS, LAM_SUM, LAM_EXP, NLAM, POWER, STATS = 80, 84, 88, 96, 128, 160, 164, 168, 170, 172

        def sm(col, n=1):
            return small[:, col:col + n]

        def ss_of(s, n):
            return sm(HEAD_SS + 16 * s, n)

        def rs_of(s, n):
            return sm(HEAD_RS + 16 * s, n)

        def tab(tt, q, which, at, d):
            at += ((tt * 2 + q) * 2 + which) * 96
            return tabs[:, at:at + d]

        landed = [sem(f"landed{i}", 16) for i in range(RAW)]
        start_loads = {n: sem(f"loaded_{n}", 16) for n in (
            "rows", "x", "ctx", "tab", "mask", "gains", "lambdas", "gate_bias", "bias", "ln", "ws",
            "post", "dil_tab", "dil_mask")}
        stored = sem("stored", 16)
        bias_out = sem("bias_out", 16)
        setup_v, setup_p, setup_a, setup_t = sem("setup_v"), sem("setup_p"), sem("setup_a"), sem("setup_t")
        weights_hi, weights_lo, piece_used = sem("weights_hi"), sem("weights_lo"), sem("piece_used")
        ada_own, ada_vector = sem("ada_own"), sem("ada_vector")
        ada_summed, ada_kept = sem("ada_summed"), sem("ada_kept")
        ada_scale_made = sem("ada_scale_made")
        squares, rstd, normed = sem("squares"), sem("rstd"), sem("normed")
        tpose, scaled_v, scaled_a = sem("tpose"), sem("scaled_v"), sem("scaled_a")
        h_hi_made, h_lo_made = sem("h_hi_made"), sem("h_lo_made")
        projected = sem("projected")
        head_sq, head_sum, head_rstd = sem("head_sq"), sem("head_sum"), sem("head_rstd")
        head_scaled, rope_a, rope_b = sem("head_scaled"), sem("rope_a"), sem("rope_b")
        heads_made, heads_turned = sem("heads_made"), sem("heads_turned")
        values_kept = sem("values_kept")
        tabs_made = sem("tabs_made")
        out_scaled, added = sem("out_scaled"), sem("added")
        scores, row_max, exps, weighed = sem("scores"), sem("row_max"), sem("exps"), sem("weighed")
        probs_turned, pT_a = sem("probs_turned"), sem("pT_a")
        attended, recips, y_made = sem("attended"), sem("recips"), sem("y_made")
        diff_sum, diff_rstd, diff_normed, means = sem("diff_sum"), sem("diff_rstd"), sem("diff_normed"), sem("means")
        bias_masked = sem("bias_masked")
        stats, ln_v, ln_p, spatial, gated = sem("stats"), sem("ln_v"), sem("ln_p"), sem("spatial"), sem("gated")
        post_sum, post_v = sem("post_sum"), sem("post_v")
        dil_rope, dil_heads_made = sem("dil_rope"), sem("dil_heads_made")

        def made_heads(u):
            return (dil_heads_made if u[0] == "din" else heads_made).seen(u)

        def ada_whos(name, j):
            return (0,) if name == "ada1" and j >= 4 else (0, 1)

        def ada_at_start(name, j):
            return name == "ada0" and j < 4

        def ada_own_piece(p):
            return ada_at_start(*p[:2]) and p[2] == 0

        def ada_place(name, j):
            return ada_sums[j % 2 if ada_at_start(name, j) else 2]

        def ada_used(p):
            return ada_own.seen(p) if ada_own_piece(p) else ada_vector.seen((*p, 1, ada_whos(*p[:2])[-1]))

        bank_for, last_in_bank = {}, {}

        def take(eng, bank, *use):
            if bank in last_in_bank:
                eng.wait_ge(*freed(last_in_bank[bank]))
            last_in_bank[bank] = use
            bank_for[use] = bank
            return banks[bank]

        def bank_of(*use):
            return banks[bank_for[use]]

        def freed(use):
            kind, rest = use[0], use[1:]
            if kind == "proj":
                return freed_by(*rest)
            if kind == "norm":
                _, ph, tt, half = use
                return (scaled_v if half == 0 else scaled_a).seen((ph, tt))
            if kind == "y":
                return h_lo_made.seen(rest)
            if kind == "heads":
                return heads_turned.seen(rest)
            if kind == "spatial":
                return gated.seen(rest)
            if kind == "ws":
                return setup_a.seen("ws_turned" + str(rest[0]))
            if kind == "rows":
                return setup_v.seen("cols")
            if kind == "ada":
                return ada_kept.seen(rest)
            if kind == "score":
                return exps.seen(rest)
            if kind == "pT":
                return pT_a.seen(rest[0])
            if kind == "out":
                return y_made.seen(rest[0])
            if kind == "dscore":
                return row_max.seen(("dil", rest[0]))
            if kind == "dpT":
                return pT_a.seen(("dil", *rest))
            assert kind == "dout"
            return y_made.seen(("dil", rest[0]))

        def freed_by(ph, c, tt):
            u = (ph, c, tt)
            if ph in ("out0", "out1"):
                return out_scaled.seen(u)
            if ph == "din" and head_span(*u):
                return dil_rope.seen(u)
            return values_kept.seen(u)

        def used_last(p):
            ph, c, pair = p
            if pair == PROJ[ph][1] // 2 - 1:
                return projected.seen((ph, c, tiles_of(ph)[-1]))
            return piece_used.seen(p)

        def hT(part, ph, kt, tt):
            w = 512 if ph in ("in0", "out0", "in1") else SEQ
            return part[:, kt * w + tt * P:kt * w + (tt + 1) * P]

        def hT4(part, ph, kt0, tt):
            w = 512 if ph in ("in0", "out0", "in1") else SEQ
            return part[:, :].rearrange("p (k t) -> p k t", t=w)[:, kt0:kt0 + 4, tt * P:(tt + 1) * P]

        def head_span(ph, c, tt):
            if ph in ("in0", "in1") and c in CHUNK_HEADS:
                parts = [kept_columns(ph, c, tt, s[0], s[1]) for s in CHUNK_HEADS[c]]
                parts = [q for q in parts if q]
                return parts[0][0], sum(q[1] for q in parts)
            if ph == "din" and DIN_COLS[c] < 18 and (DIN_COLS[c] // 2) % 3 < 2:
                return 0, NC
            return None

        head_chunks = {(ph, c): n for n, (ph, c) in enumerate(
            (ph, c) for ph in ("in0", "in1", "din") for c in range(PROJ[ph][0]) if head_span(ph, c, 0))}

        def turn_slot(ph, c, tt):
            return tt if ph != "din" else (head_chunks[(ph, c)] % 2) * 2 + tt

        prob_at = {}
        for layer in range(2):
            n = 0
            for u in units_of(layer):
                for m in range(2 if u[2] == "A" else 1):
                    prob_at[(u, m)] = n
                    n += 1

        def prob_slot(layer, u, m):
            return prob_at[(u, m)] % 4

        def dil_score_place(i, g):
            nk = (i % 2 + 1) * P
            return (g * nk, 0) if nk == P or g < 2 else (0, 1)

        def rope_product(eng, to, source, off, pitch, w, d, table):
            h = d // 2
            turned = bass.AP(source, off + h, [[pitch, P], [d, w // d], [-h, 2], [1, h]])
            return eng.tensor_tensor(to.rearrange("p (n a h) -> p n a h", a=2, h=h), turned,
                                     table.rearrange("p (a h) -> p a h", a=2).unsqueeze(1).broadcast_to([P, w // d, 2, h]),
                                     ALU.mult)

        def norm_scale(ph, kt, who):
            if ph in ("in0", "in1"):
                return a_scale[:, kt, who:who + 1]
            return cols[:, (32 if ph == "gin" else 40) + kt:(33 if ph == "gin" else 41) + kt]

        def step_before(u, back):
            ph, c, tt = u
            if ph in ("in0", "in1"):
                order = [(ph, cc, t) for cc in range(7) for t in tiles_of(ph) if head_span(ph, cc, t)]
                i = order.index(u)
                return order[i - back] if i >= back else None
            order = [(ph, cc, t) for cc in range(20) for t in X_TILES if head_span(ph, cc, t)]
            i = order.index(u)
            return order[i - back] if i >= back else None

        def prob_user(layer, n):
            for (u, m), k in prob_at.items():
                if u[0] == layer and k == n:
                    return u, m
            raise AssertionError

        def prob_free(layer, n):
            u, m = prob_user(layer, n)
            return weighed.seen(u) if m else probs_turned.seen(u)

        def value_columns(kind, h):
            first, pair = {"A": (0, h // 2), "B": (256, 0), "C": (384, h // 2)}[kind]
            return first + pair * P, (h // 3 if kind == "B" else h % 2) * HD

        def head_output(u):
            at = value_columns(*u[2:])[1]
            return bank_of("out", u)[:, at:at + HD]

        def nm_col(u, m):
            return sm(NM + prob_at[(u, m)] % 4)

        def z_col(u, m):
            k = Z + 2 * (prob_at[(u, m)] % 4)
            return sm(k), sm(k + 1)

        block = ctx.enter_context(nc.Block())

        def weight_source(p):
            ph, c, pair = p
            if ph.startswith("ada"):
                src, col = a["w_ada"][int(ph[3])], c * NC
            elif ph in ("in0", "in1"):
                src, col = a["w_in"][int(ph[2])], c * NC
            elif ph in ("out0", "out1"):
                src, col = a["w_out"][int(ph[3])], c * NC
            elif ph == "gin":
                src, col = a["a_w_in_2"][0], GIN_COLS[c] * NC
            elif ph == "gout":
                src, col = a["a_w_out_2"][0], c * NC
            elif ph == "din":
                src, col = a["b_w_in_2"][0], DIN_COLS[c] * NC
            else:
                src, col = a["b_w_out_2"][0], c * NC
            return src[pair * 2 * P:(pair + 1) * 2 * P, col:col + NC].rearrange("(k p) n -> p k n", p=P)

        @block.sync
        def _(sp):
            sp.dma_start(rows[0:8, :], a["c"].rearrange("b (k p) -> (b k) p", p=P)).then_inc(*start_loads["rows"].at(0))
            sp.dma_start(rows[8:16, :], a["c_ctx"].rearrange("(k p) -> k p", p=P)).then_inc(*start_loads["rows"].at(1))
            sp.dma_start(rows[16:32, :], a["norm_g"].rearrange("l (k p) -> (l k) p", p=P)).then_inc(*start_loads["rows"].at(2))
            sp.dma_start(rows[32:48, :], a["norm_pre_2"].rearrange("l (k p) -> (l k) p", p=P)).then_inc(*start_loads["rows"].at(3))
            sp.dma_start(rows[48:56, :], a["a_b_s_2"][0]).then_inc(*start_loads["rows"].at(4))
            sp.dma_start(rows[56:ROWS, :], a["b_ada"].rearrange("l (k p) -> (l k) p", p=P)).then_inc(*start_loads["rows"].at(5))
            for n, p in enumerate(PIECES):
                if n >= RAW:
                    was = PIECES[n - RAW]
                    if was[0].startswith("ada"):
                        sp.wait_ge(*ada_used(was))
                    else:
                        sp.wait_ge(*weights_hi.seen(was))
                        sp.wait_ge(*weights_lo.seen(was))
                sp.dma_start(raw[:, n % RAW, :, :], weight_source(p)).then_inc(*landed[n % RAW].at(p))
                if n == 2:
                    sp.dma_start(x[:, 0:2, :], a["x"][0].rearrange("(t p) d -> p t d", p=P)).then_inc(*start_loads["x"].at(0))
                    sp.dma_start(x[:, 2:4, :], a["ctx"][0].rearrange("(t p) d -> p t d", p=P)).then_inc(*start_loads["ctx"].at(0))
            o = out[0].rearrange("(t p) d -> t p d", p=P)
            for tt in X_TILES:
                sp.wait_ge(*added.seen(("dout", 1, tt)))
                sp.dma_start(o[tt], x[:, tt, :]).then_inc(*stored.at(tt))
            sp.wait_ge(*stored.seen(1))

        @block.tensor
        def _(pe):
            ring = [0]

            def ada_own_products(j):
                p = ("ada0", j, 0)
                bank = take(pe, (TURN_BANK, OUT_BANK)[j % 2], "ada", "ada0", j)
                pe.wait_ge(*landed[PIECE_AT[p] % RAW].seen(p))
                for k in range(2):
                    for i in range(4):
                        mm = pe.matmul(bank[:, 2 * i:2 * i + 2], raw[:, PIECE_AT[p] % RAW, k, i * P:(i + 1) * P], cvec[:, k, :],
                                       start=(k == 0 and i == 0), stop=False)
                mm.then_inc(*ada_own.at(p))

            def ada_total(name, j):
                if j < 4:
                    own = ada_at_start(name, j)
                    bank = bank_of("ada", name, j) if own else take(pe, TURN_BANK, "ada", name, j)
                    pe.wait_ge(*ada_used((name, j, 3)))
                    for i in range(4):
                        for who in range(2):
                            mm = pe.matmul(bank[:, 2 * i + who:2 * i + who + 1], ada_place(name, j)[:, who, i * P:(i + 1) * P], ones[:, 0:1],
                                           start=(i == 0 and who == 0 and not own), stop=(i == 3 and who == 1))
                    mm.then_inc(*ada_summed.at((name, j)))
                    return
                pe.wait_ge(*ada_used((name, j, 3)))
                for who in ada_whos(name, j):
                    bank = take(pe, (TURN_BANK, OUT_BANK)[who], "ada", name, j, who)
                    pe.matmul(bank[:, :], ones[:, :], ada_place(name, j)[:, who, :], start=True, stop=True).then_inc(*ada_summed.at((name, j, who)))

            turned = set()

            def norm_turns(ph, tt):
                turned.add((ph, tt))
                pe.wait_ge(*normed.seen((ph, tt)))
                for half in range(2):
                    bank = take(pe, 6 + half, "norm", ph, tt, half)
                    for i in range(4):
                        kt = half * 4 + i
                        mm = pe.transpose(bank[:, i * P:(i + 1) * P], xn[tt % 2][:, kt * P:(kt + 1) * P], ident[:, :])
                    mm.then_inc(*tpose.at((ph, tt, half)))

            def y_turn(ph, src, tt, q):
                bank = take(pe, 6 + (tt if ph == "gout" else q) % 2, "y", ph, tt, q)
                for i in range(4):
                    kt = q * 4 + i
                    mm = pe.transpose(bank[:, i * P:(i + 1) * P], src[:, tt, kt * P:(kt + 1) * P], ident[:, :])
                mm.then_inc(*tpose.at((ph, tt, q)))

            def product(ph, c, p, k, tt):
                kts = PROJ[ph][1]
                kt = p[2] * 2 + k
                s = SPLIT_AT[p] % SPLIT
                if kt == 0:
                    n = 4 if ph in BESIDE else 6
                    take(pe, ring[0] % n, "proj", ph, c, tt)
                    ring[0] += 1
                if c == 0 and kt % 4 == 0:
                    pe.wait_ge(*h_hi_made.seen((ph, tt, kt // 4)))
                    pe.wait_ge(*h_lo_made.seen((ph, tt, kt // 4)))
                lo, w = columns_of(ph, c, tt)
                bank = bank_of("proj", ph, c, tt)[:, lo:lo + w]
                first, last = kt == 0, kt == kts - 1
                pe.matmul(bank, hT(h_hi, ph, kt, tt), w_lo[:, s, k, lo:lo + w], start=first, stop=False)
                pe.matmul(bank, hT(h_lo, ph, kt, tt), w_hi[:, s, k, lo:lo + w], start=False, stop=False)
                mm = pe.matmul(bank, hT(h_hi, ph, kt, tt), w_hi[:, s, k, lo:lo + w], start=False, stop=last)
                if last:
                    mm.then_inc(*projected.at((ph, c, tt)))
                elif k == 1 and tt == tiles_of(ph)[-1]:
                    mm.then_inc(*piece_used.at(p))

            def weights(p):
                pe.wait_ge(*weights_hi.seen(p))
                pe.wait_ge(*weights_lo.seen(p))

            def head_turn(ph, c, tt):
                span = head_span(ph, c, tt)
                if span is None:
                    return
                pe.wait_ge(*made_heads((ph, c, tt)))
                bank = take(pe, TURN_BANK, "heads", ph, c, tt)
                t = heads[turn_slot(ph, c, tt)]
                for i in range(span[0] // P, (span[0] + span[1]) // P):
                    mm = pe.transpose(bank[:, i * P:(i + 1) * P], t[:, i * P:(i + 1) * P], ident[:, :])
                mm.then_inc(*tpose.at(("heads", ph, c, tt)))

            def project(ph, between=None, after_piece=None):
                tts = tiles_of(ph)
                pairs = PROJ[ph][1] // 2
                for c in range(PROJ[ph][0]):
                    pieces = [(ph, c, pair) for pair in range(pairs)]
                    if c == 0 and pairs <= SPLIT:
                        normed_first = ph in ("in0", "in1", "gin", "din")
                        for tt in tts:
                            for p in pieces:
                                if p == pieces[-1] and normed_first and tt + 1 in tts and (ph, tt + 1) not in turned:
                                    norm_turns(ph, tt + 1)
                                if tt == tts[0]:
                                    weights(p)
                                for k in range(2):
                                    product(ph, c, p, k, tt)
                        if between:
                            between(c)
                        continue
                    ending = pieces[-SPLIT:] if ph in FOLLOWING and c == PROJ[ph][0] - 1 else []
                    for n, p in enumerate(pieces):
                        if p in ending:
                            continue
                        weights(p)
                        for k in range(2):
                            for tt in tts:
                                product(ph, c, p, k, tt)
                            tt = TURNED_AFTER.get((n, k))
                            if c and tt in tts:
                                head_turn(ph, c - 1, tt)
                            if k == 0 and after_piece:
                                after_piece((p, 0))
                        if p in ADA_READY:
                            ada_total(*ADA_READY[p])
                        if after_piece:
                            after_piece((p, 1))
                    for tt in tts if ending else ():
                        if tt == 3:
                            norm_turns(FOLLOWING[ph], 0)
                        for p in ending:
                            if tt == tts[0]:
                                weights(p)
                            if tt == tts[-1] and p == ending[-1] and FOLLOWING[ph]:
                                norm_turns(FOLLOWING[ph], 1 if tt == 3 else 0)
                            for k in range(2):
                                product(ph, c, p, k, tt)
                    if between:
                        between(c)

            def attention1(layer):
                units = units_of(layer)
                solo = len(steps_beside(f"in{layer}"))
                ph = f"in{layer}"
                fill = fill_of(layer)
                s_use = [0]

                def score(u, i):
                    _, qt, kind, h = u
                    k0 = 0 if qt in X_TILES else 256
                    c = {"A": 0, "B": 2, "C": 5}[kind]
                    if h == 0 and qt == 0:
                        for cc in ([4, 5] if kind == "C" else [c]):
                            for tt in ALL_TILES:
                                pe.wait_ge(*heads_turned.seen((ph, cc, tt)))
                    for m in range(2 if kind == "A" else 1):
                        n = s_use[0]
                        s_use[0] += 1
                        ring = SCORE_BANKS if i < solo else SCORE_BANKS + (2, 3)
                        bank = take(pe, ring[n % len(ring)], "score", layer, n)
                        if kind == "A":
                            col = (2 * h + m) * 32
                            tq, tk, base, d = col // P, 2 + col // P, col % P, 32
                        elif kind == "B":
                            tq, tk, base, d = 4 + h % 3, 7, (h // 3) * HD, HD
                        else:
                            tq, tk, base, d = 8 + h // 2, 11 + h // 2, (h % 2) * HD, HD
                        mm = pe.matmul(bank[:, k0:512], qkT[base:base + d, tq, qt * P:(qt + 1) * P],
                                       qkT[base:base + d, tk, k0:512], start=True, stop=True)
                        mm.then_inc(*scores.at((u, m)))

                def turn(i):
                    u = units[i]
                    pe.wait_ge(*(weighed.seen(u) if u[2] == "A" else exps.seen((layer, prob_at[(u, 0)]))))
                    bank = take(pe, TURN_BANK if i + 1 < solo or i % 2 else 0, "pT", u)
                    kt0 = 0 if u[1] in X_TILES else 2
                    for j in range(kt0, 4):
                        mm = pe.transpose(bank[:, j * P:(j + 1) * P], probs[prob_slot(layer, u, 0)][:, j * P:(j + 1) * P], ident[:, :])
                    mm.then_inc(*probs_turned.at(u))

                def attend(i):
                    u = units[i]
                    _, qt, kind, h = u
                    if h == 0 and qt == 0:
                        c = {"A": 1, "B": 3, "C": 6}[kind]
                        for tt in ALL_TILES:
                            pe.wait_ge(*values_kept.seen((ph, c, tt)))
                    pe.wait_ge(*pT_a.seen(u))
                    bank = take(pe, OUT_BANK if i + 2 < solo or i % 2 else 1, "out", u)
                    vcol, _ = value_columns(kind, h)
                    kt0 = 0 if qt in X_TILES else 2
                    for j in range(kt0, 4):
                        mm = pe.matmul(bank[:, 0:P], pT[i % 2][:, j * P:(j + 1) * P],
                                       vals[:, j, vcol:vcol + P], start=(j == kt0), stop=(j == 3))
                    mm.then_inc(*attended.at(u))

                def step(i):
                    if i == 0:
                        score(units[0], 0)
                    if i + 1 < len(units):
                        score(units[i + 1], i)
                    for task in fill.get(i, ()):
                        if task[0] == "ada":
                            ada_total(*task[1:])
                    if 0 <= i - 1 < len(units):
                        turn(i - 1)
                    if i >= 2:
                        attend(i - 2)
                    for task in fill.get(i, ()):
                        if task[0] == "y":
                            if task[1] == 0:
                                for qt in (ALL_TILES if layer == 0 else X_TILES):
                                    pe.wait_ge(*diff_normed.seen((layer, qt)))
                                    pe.wait_ge(*y_made.seen((layer, qt, "B", B_HEADS - 1)))
                            y_turn(f"out{layer}", gate, task[1], 0)

                return step, solo, len(units)

            def attention2():
                solo = len(steps_beside("din"))
                units = [(qt, h) for h in range(DIL_HEADS) for qt in X_TILES]
                s_use = [0]

                def score(i):
                    qt, h = units[i]
                    if h in (0, DIL_HEADS // 2) and qt == 0:
                        for c in ([7, 6, 4, 3, 1, 0] if h == 0 else [18, 17, 15, 14, 12, 11]):
                            for tt in X_TILES:
                                pe.wait_ge(*heads_turned.seen(("din", c, tt)))
                    nk = (qt + 1) * P
                    base = (h % 2) * HD
                    ring = SCORE_BANKS if i <= solo else SCORE_BANKS + (2, 3)
                    for g in range(DIL):
                        at, second = dil_score_place(i, g)
                        if g == 0 or second:
                            bank = take(pe, ring[s_use[0] % len(ring)], "dscore", i, second)
                            s_use[0] += 1
                        mm = pe.matmul(bank[:, at:at + nk], dqkT[base:base + HD, g * 16 + h // 2, qt * P:(qt + 1) * P],
                                       dqkT[base:base + HD, g * 16 + 8 + h // 2, 0:nk], start=True, stop=True)
                    mm.then_inc(*scores.at(("dil", i)))

                def turn(i, part):
                    n = DIL * (i % 2 + 1)
                    lo = 4 * part
                    if lo < n:
                        pe.wait_ge(*exps.seen(("dil", i)))
                        bank = take(pe, TURN_BANK if i + 1 < solo or (i + part) % 2 else 0, "dpT", i, part)
                        for t in range(lo, min(lo + 4, n)):
                            mm = pe.transpose(bank[:, (t - lo) * P:(t - lo + 1) * P], probs2[i % 3][:, t * P:(t + 1) * P], ident[:, :])
                        mm.then_inc(*probs_turned.at(("dil", i, part)))

                def attend(i):
                    qt, h = units[i]
                    if h in (0, DIL_HEADS // 2) and qt == 0:
                        for c in ([8, 5, 2] if h == 0 else [19, 16, 13]):
                            for tt in X_TILES:
                                pe.wait_ge(*values_kept.seen(("din", c, tt)))
                    for part in range(qt + 1):
                        pe.wait_ge(*freed(("dpT", i, part)))
                    bank = take(pe, OUT_BANK if i + 2 < solo or i % 2 else 1, "dout", i)
                    n = DIL * (qt + 1)
                    for t in range(n):
                        g, kt = t // (qt + 1), t % (qt + 1)
                        mm = pe.matmul(bank[:, 0:P], pT2[i % 2][:, t * P:(t + 1) * P],
                                       dvals[:, kt, g, h // 2 * P:(h // 2 + 1) * P], start=(t == 0), stop=(t == n - 1))
                    mm.then_inc(*attended.at(("dil", i)))

                def step(i):
                    if i == 0:
                        score(0)
                    if i + 1 < len(units):
                        score(i + 1)
                    if 0 <= i - 1 < len(units):
                        turn(i - 1, 0)
                    if i >= 2:
                        attend(i - 2)
                    if 0 <= i - 1 < len(units):
                        turn(i - 1, 1)

                return step, solo, len(units)

            def project_with(ph, attention):
                step, solo, units = attention
                slots = steps_beside(ph)
                project(ph, None, lambda p: step(slots[p]) if p in slots else None)
                for i in range(solo, units + 2):
                    step(i)

            pe.wait_ge(*setup_p.seen("ident"))
            pe.wait_ge(*start_loads["rows"].seen(5))
            bank = take(pe, 6, "rows")
            pe.transpose(bank[:, 0:ROWS], rows[:, :], ident[0:ROWS, 0:ROWS]).then_inc(*setup_t.at("rows"))
            pe.wait_ge(*setup_a.seen("cvec"))
            pe.wait_ge(*setup_p.seen("ones"))
            ada_own_products(0)
            for j in range(4):
                if j < 3:
                    ada_own_products(j + 1)
                ada_total("ada0", j)
            norm_turns("in0", 0)
            project_with("in0", attention1(0))
            for layer in range(2):
                ph = f"out{layer}"
                for u in units_of(layer)[-2:]:
                    pe.wait_ge(*y_made.seen(u))
                for tt in tiles_of(ph):
                    y_turn(ph, gate, tt, 1)
                project(ph)
                if layer == 0:
                    project_with("in1", attention1(1))

            def spatial_step(c):
                if c == 0:
                    pe.wait_ge(*setup_p.seen("ws"))
                    for half in range(2):
                        bank = take(pe, 6 + half, "ws", half)
                        for i in range(4):
                            mm = pe.transpose(bank[:, i * P:(i + 1) * P], ws_raw[:, half * 4 + i, :], ident[:, :])
                        mm.then_inc(*tpose.at(("ws", half)))
                if 6 <= c <= 9:
                    j = c - 6
                    if j == 0:
                        pe.wait_ge(*ln_p.seen(0))
                        pe.wait_ge(*ln_p.seen(1))
                        pe.wait_ge(*setup_a.seen("ws_turned1"))
                    for tt in X_TILES:
                        bank = take(pe, 6 + tt, "spatial", j, tt)
                        for i in range(2):
                            g = 2 * j + i
                            mm = pe.matmul(bank[:, i * 256:(i + 1) * 256], ws_T[:, g, :], gv[:, tt, g * 256:(g + 1) * 256],
                                           start=True, stop=True)
                        mm.then_inc(*spatial.at((j, tt)))

            project("gin", spatial_step)
            for q in range(4):
                for tt in X_TILES:
                    pe.wait_ge(*gated.seen(("z", q, tt)))
                    y_turn("gout", gu, tt, q)
            project("gout")
            project_with("din", attention2())
            for i in (30, 31):
                pe.wait_ge(*y_made.seen(("dil", i)))
            for tt in X_TILES:
                for q in range(2):
                    y_turn("dout", dgate, tt, q)
            project("dout")

        @block.scalar
        def _(act):
            at = [0]

            def split_until(n):
                for i in range(at[0], min(n, len(SPLITS))):
                    p = SPLITS[i]
                    act.wait_ge(*landed[PIECE_AT[p] % RAW].seen(p))
                    if i >= SPLIT:
                        act.wait_ge(*used_last(SPLITS[i - SPLIT]))
                    act.activation(w_hi[:, i % SPLIT, :, :], raw[:, PIECE_AT[p] % RAW, :, :], ACT.Copy) \
                        .then_inc(*weights_hi.at(p))
                at[0] = max(at[0], n)

            def square(ph, tt, half):
                act.activation(junk, x[:, tt, half * NC:(half + 1) * NC], ACT.Square, accum_out=sm(SS + 2 * tt + half)) \
                    .then_inc(*squares.at((ph, tt, half)))
                act.wait_ge(*squares.seen((ph, tt, half)))

            def norm_tile(ph, tt):
                bias = ph in ("in0", "in1")
                v = vt[tt % 2]
                act.wait_ge(*tpose.seen((ph, tt, 1)))
                if tt >= 2:
                    act.wait_ge(*h_lo_made.seen((ph, tt - 2, 1)))
                if bias and tt == 0:
                    act.wait_ge(*ada_scale_made.seen(ph))
                for i in range(4):
                    kt = 4 + i
                    who = 0 if tt in X_TILES else 1
                    ins = act.activation(v[:, kt * P:(kt + 1) * P], bank_of("norm", ph, tt, 1)[:, i * P:(i + 1) * P],
                                         ACT.Identity, scale=norm_scale(ph, kt, who),
                                         bias=ada_cols[:, kt, who:who + 1] if bias else 0.0)
                ins.then_inc(*scaled_a.at((ph, tt)))
                act.wait_ge(*scaled_v.seen((ph, tt)))
                for half in range(2):
                    if half == 1:
                        act.wait_ge(*scaled_a.seen((ph, tt)))
                    act.activation(hT4(h_hi, ph, half * 4, tt), v[:, half * 512:(half + 1) * 512].rearrange("p (k t) -> p k t", k=4),
                                   ACT.Copy).then_inc(*h_hi_made.at((ph, tt, half)))

            def end_of(ph, process_tile, squares_of):
                following, tts = FOLLOWING[ph], tiles_of(ph)
                for tt in tts[:-1]:
                    process_tile(tt)
                    squares_of(tt)
                first = SPLIT_AT[(following, 0, 0)]
                if len(tts) == 4:
                    norm_tile(following, 0)
                split_until(first + SPLIT - 1)
                if len(tts) == 2:
                    norm_tile(following, 0)
                process_tile(tts[-1])
                squares_of(tts[-1])
                split_until(first + SPLIT)
                for tt in tiles_of(following)[1:]:
                    norm_tile(following, tt)

            def y_part(ph, tt, q):
                act.wait_ge(*tpose.seen((ph, tt, q)))
                act.activation(hT4(h_hi, ph, q * 4, tt), bank_of("y", ph, tt, q)[:, :].rearrange("p (k t) -> p k t", k=4),
                               ACT.Copy).then_inc(*h_hi_made.at((ph, tt, q)))

            def process_in(ph, c, beside):
                for tt in tiles_of(ph):
                    u = (ph, c, tt)
                    bank = bank_of("proj", *u)
                    span = head_span(*u)
                    act.wait_ge(*projected.seen(u))
                    steps = []
                    if c in CHUNK_VALUES:
                        col, n, place = CHUNK_VALUES[c]
                        steps.append((vals[:, tt, place:place + n], bank[:, col:col + n], ACT.Copy))
                    if c in CHUNK_GATES:
                        col, n, place = CHUNK_GATES[c]
                        if kept_columns(ph, c, tt, col, n):
                            steps.append((gate[:, tt, place:place + n], bank[:, col:col + n], ACT.Silu))
                    if span:
                        before = step_before(u, 4)
                        if before:
                            act.wait_ge(*tpose.seen(("heads", *before)))
                        a_, b_ = span[0], span[0] + span[1]
                        if c == 2 and a_ == 0:
                            a_ = 384
                            steps.append((heads[tt][:, 0:a_].rearrange("p (i k d) -> p k i d", k=B_KV, d=HD),
                                          bank[:, 0:a_].rearrange("p (k i d) -> p k i d", k=B_KV, d=HD), ACT.Copy))
                        steps.append((heads[tt][:, a_:b_], bank[:, a_:b_], ACT.Copy))
                    for out_ap, in_ap, f in steps:
                        last = act.activation(out_ap, in_ap, f)
                    last.then_inc(*values_kept.at(u))
                    if tt == 1:
                        beside()
                square_heads(ph, c, 0)
                square_heads(ph, c, 1)

            def square_heads(ph, c, k):
                if ph == "din" or c < 0 or k >= len(tiles_of(ph)):
                    return
                u = (ph, c, tiles_of(ph)[k])
                span = head_span(*u)
                if span:
                    before = step_before(u, 1)
                    if before:
                        act.wait_ge(*head_sum.seen(before))
                    act.wait_ge(*values_kept.seen(u))
                    a_, b_ = span[0], span[0] + span[1]
                    act.activation(sq[:, a_:b_], heads[u[2]][:, a_:b_], ACT.Square).then_inc(*head_sq.at(u))

            def turned_heads(ph, c, tt):
                span = head_span(ph, c, tt)
                if not span:
                    return
                act.wait_ge(*tpose.seen(("heads", ph, c, tt)))
                t0, n = span[0] // P, span[1] // P
                if ph == "din":
                    col = DIN_COLS[c]
                    tile0 = (col // 6) * 16 + ((col // 2) % 3) * 8 + (col % 2) * 4
                    dst = dqkT
                else:
                    tile0 = CHUNK_TILE0[c]
                    dst = qkT
                act.activation(dst[:, tile0 + t0:tile0 + t0 + n, tt * P:(tt + 1) * P],
                               bank_of("heads", ph, c, tt)[:, t0 * P:(t0 + n) * P].rearrange("p (k t) -> p k t", k=n),
                               ACT.Copy).then_inc(*heads_turned.at((ph, c, tt)))

            def project(ph, process, after_piece=None):
                pairs = PROJ[ph][1] // 2
                tts = tiles_of(ph)
                limit = SPLIT_AT[(ph, 0, 0)] + PROJ[ph][0] * pairs if ph == "in0" else len(SPLITS)
                for c in range(PROJ[ph][0] - (1 if FOLLOWING.get(ph) and pairs <= SPLIT else 0)):
                    for n in range(pairs):
                        p = (ph, c, n)
                        if ph in FOLLOWING and c == PROJ[ph][0] - 1 and n >= pairs - SPLIT:
                            continue
                        if c and TURNED_AFTER.get((n, 0)) in tts:
                            turned_heads(ph, c - 1, TURNED_AFTER[(n, 0)])
                        if after_piece:
                            after_piece((p, 0))
                        if ph in ("in0", "in1"):
                            square_heads(ph, c - 1, n + 2)
                        if n < pairs - 1:
                            split_until(min(limit, SPLIT_AT[p] + SPLIT + 1))
                        if c and TURNED_AFTER.get((n, 1)) in tts:
                            turned_heads(ph, c - 1, TURNED_AFTER[(n, 1)])
                        if n < pairs - 1 or not after_piece:
                            if n == pairs - 1:
                                split_until(min(limit, SPLIT_AT[p] + SPLIT + (1 if ph in FOLLOWING else 0)))
                                process(ph, c)
                                split_until(min(limit, SPLIT_AT[p] + SPLIT + 1))
                        else:
                            process(ph, c, lambda: after_piece((p, 1)))
                            split_until(min(limit, SPLIT_AT[p] + SPLIT + 1))
                            continue
                        if after_piece:
                            after_piece((p, 1))

            def attention1(layer):
                units = units_of(layer)
                fill = fill_of(layer)
                n_use = [0]

                def expo(u):
                    _, qt, kind, h = u
                    k0 = 0 if qt in X_TILES else 256
                    for m in range(2 if kind == "A" else 1):
                        n = n_use[0]
                        n_use[0] += 1
                        bank = bank_of("score", layer, n)
                        slot = prob_slot(layer, u, m)
                        zc = z_col(u, m)
                        act.wait_ge(*row_max.seen((u, m)))
                        if n >= 4:
                            act.wait_ge(*prob_free(layer, n - 4))
                            act.wait_ge(*recips.seen(prob_user(layer, n - 4)[0]))
                        if kind == "C" and qt in X_TILES:
                            act.activation(probs[slot][:, 0:256], probs[slot][:, 0:256], ACT.Exp, scale=-1.0,
                                           bias=nm_col(u, m), accum_out=zc[0])
                            act.activation(probs[slot][:, 256:512], bank[:, 256:512], ACT.Exp, bias=nm_col(u, m),
                                           accum_out=zc[1]).then_inc(*exps.at((layer, n)))
                        else:
                            act.activation(probs[slot][:, k0:512], bank[:, k0:512], ACT.Exp, bias=nm_col(u, m),
                                           accum_out=zc[0]).then_inc(*exps.at((layer, n)))

                def keep_turned(i):
                    u = units[i]
                    k0 = 0 if u[1] in X_TILES else 256
                    act.wait_ge(*probs_turned.seen(u))
                    if i >= 2:
                        act.wait_ge(*attended.seen(units[i - 2]))
                    act.activation(pT[i % 2][:, k0:512], bank_of("pT", u)[:, k0:512], ACT.Copy).then_inc(*pT_a.at(u))

                def diff_squares(i):
                    u = units[i]
                    if u[2] == "A":
                        key = (layer, u[1], u[3])
                        act.wait_ge(*attended.seen(u))
                        act.wait_ge(*recips.seen(u))
                        if i:
                            act.wait_ge(*diff_sum.seen((layer, units[i - 1][1], units[i - 1][3])))
                        act.activation(bank_of("out", u)[:, 2 * P:2 * P + HD], head_output(u), ACT.Square, scale=sm(RZ + prob_at[(u, 0)] % 8),
                                       accum_out=sm(DIFF_SS + 4 * u[1] + u[3])).then_inc(*diff_sum.at(key))

                def step(i):
                    if i == 0:
                        expo(units[0])
                    if 0 <= i - 1 < len(units):
                        keep_turned(i - 1)
                    if i + 1 < len(units):
                        expo(units[i + 1])
                    if i >= 2:
                        diff_squares(i - 2)
                    for task in fill.get(i, ()):
                        if task[0] == "y":
                            y_part(f"out{layer}", task[1], 0)
                        if task[0] == "split":
                            split_until(SPLIT_AT[(f"out{layer}", 0, 0)] + task[1] + 1)

                return step, len(steps_beside(f"in{layer}")), len(units)

            def project_with(ph, process, attention):
                step, solo, units = attention
                slots = steps_beside(ph)
                project(ph, process, lambda p: step(slots[p]) if p in slots else None)
                for i in range(solo, units + 2):
                    step(i)

            act.wait_ge(*setup_v.seen("cols"))
            act.activation(cvec[:, :, 0], cols[:, 0:8], ACT.Silu)
            act.activation(cvec[:, :, 1], cols[:, 8:16], ACT.Silu).then_inc(*setup_a.at("cvec"))
            for tt in ALL_TILES:
                act.wait_ge(*start_loads["x" if tt in X_TILES else "ctx"].seen(0))
                for half in range(2):
                    square("in0", tt, half)
            norm_tile("in0", 0)
            split_until(SPLIT)
            for tt in ALL_TILES[1:]:
                norm_tile("in0", tt)
            act.wait_ge(*setup_v.seen("lambda_sums"))
            act.activation(sm(LAM_EXP, 4), sm(LAM_SUM, 4), ACT.Exp).then_inc(*setup_a.at("lambda_exp"))
            project_with("in0", process_in, attention1(0))
            for layer in range(2):
                ph = f"out{layer}"
                for tt in tiles_of(ph):
                    y_part(ph, tt, 1)
                following = FOLLOWING[ph]
                project(ph, lambda ph, c: None)
                for tt in tiles_of(following):
                    act.wait_ge(*added.seen((ph, 0, tt)))
                    square(following, tt, 0)

                def last_squares(tt):
                    if tt in tiles_of(following):
                        act.wait_ge(*added.seen((ph, 1, tt)))
                        square(following, tt, 1)

                end_of(ph, lambda tt: None, last_squares)
                if layer == 0:
                    project_with("in1", process_in, attention1(1))

            def process_gin(ph, c):
                if c == 1:
                    for half in range(2):
                        act.wait_ge(*tpose.seen(("ws", half)))
                        act.activation(ws_T[:, half * 4:half * 4 + 4, :], bank_of("ws", half)[:, :].rearrange("p (g t) -> p g t", g=4),
                                       ACT.Copy).then_inc(*setup_a.at("ws_turned" + str(half)))
                for tt in X_TILES:
                    u = (ph, c, tt)
                    act.wait_ge(*projected.seen(u))
                    bank = bank_of("proj", *u)
                    if c < 4:
                        act.activation(gv[:, tt, c * NC:(c + 1) * NC], bank[:, :], ACT.Gelu).then_inc(*values_kept.at(u))
                    elif c < 8:
                        act.activation(gu[:, tt, (c - 4) * NC:(c - 3) * NC], bank[:, :], ACT.Gelu).then_inc(*values_kept.at(u))
                    else:
                        j = (c - 8) * 2 + tt
                        if j >= 4:
                            act.wait_ge(*gated.seen(("z", (j - 4) // 2, (j - 4) % 2)))
                        act.activation(silu_z[j % 4], bank[:, :], ACT.Silu).then_inc(*values_kept.at(u))

            project("gin", process_gin)
            for q in range(4):
                for tt in X_TILES:
                    y_part("gout", tt, q)

            def post_tile(ph, c, tt):
                u = (ph, c, tt)
                act.wait_ge(*projected.seen(u))
                bank = bank_of("proj", *u)
                act.activation(y_out[:, tt, c * NC:(c + 1) * NC], bank[:, :], ACT.Copy)
                prev = (ph, c, tt - 1) if tt else (ph, c - 1, 1)
                if prev[1] >= 0:
                    act.wait_ge(*values_kept.seen(prev))
                act.activation(junk, bank[:, :], ACT.Square, accum_out=sm(POST_SS + 2 * tt + c)) \
                    .then_inc(*values_kept.at(u))

            def process_post(ph, c):
                for tt in X_TILES:
                    post_tile(ph, c, tt)

            def squares_after_post(tt):
                act.wait_ge(*added.seen(("gout", 1, tt)))
                for half in range(2):
                    square("din", tt, half)

            project("gout", process_post)
            end_of("gout", lambda tt: post_tile("gout", 1, tt), squares_after_post)

            def process_din(ph, c, beside):
                col = DIN_COLS[c]
                for tt in X_TILES:
                    u = (ph, c, tt)
                    if tt == 1:
                        beside()
                    if head_span(*u):
                        continue
                    act.wait_ge(*projected.seen(u))
                    src = bank_of("proj", *u)[:, :]
                    if col >= 18:
                        act.activation(dgate[:, tt, (col - 18) * NC:(col - 17) * NC], src, ACT.Silu).then_inc(*values_kept.at(u))
                    else:
                        act.activation(dvals[:, tt, col // 6, (col % 2) * NC:(col % 2 + 1) * NC], src, ACT.Copy) \
                            .then_inc(*values_kept.at(u))

            def dil_exp(i):
                n = DIL * P * (i % 2 + 1)
                act.wait_ge(*row_max.seen(("dil", i)))
                act.activation(probs2[i % 3][:, 0:n], probs2[i % 3][:, 0:n], ACT.Exp, scale=-1.0,
                               bias=sm(DNM + i % 4), accum_out=sm(DZ + i % 4)).then_inc(*exps.at(("dil", i)))

            def dil_keep(i):
                for part in range(i % 2 + 1):
                    act.wait_ge(*probs_turned.seen(("dil", i, part)))
                    if i >= 2:
                        act.wait_ge(*attended.seen(("dil", i - 2)))
                    lo, n = (512, 256) if part else (0, 512 if i % 2 else 384)
                    act.activation(pT2[i % 2][:, lo:lo + n], bank_of("dpT", i, part)[:, 0:n], ACT.Copy).then_inc(*pT_a.at(("dil", i, part)))

            def dil_step(i):
                if i == 0:
                    dil_exp(0)
                if 0 <= i - 1 < 32:
                    dil_keep(i - 1)
                if i < 31:
                    dil_exp(i + 1)

            project_with("din", process_din, (dil_step, len(steps_beside("din")), 32))
            for tt in X_TILES:
                for q in range(2):
                    y_part("dout", tt, q)
            project("dout", process_post)
            process_post("dout", 1)

        @block.gpsimd
        def _(pool):
            pool.memset(ident[:, :], 0.0).then_inc(*setup_p.at("zero"))
            pool.memset(ones[:, :], 1.0).then_inc(*setup_p.at("ones"))
            pool.wait_ge(*setup_p.seen("zero"))
            pool.affine_select(out=ident[:, :], in_=ident[:, :], compare_op=ALU.not_equal, fill=1.0, base=0,
                               pattern=[[-1, P]], channel_multiplier=1).then_inc(*setup_p.at("ident"))
            pool.memset(sm(POWER), -0.5).then_inc(*setup_p.at("power"))
            half = sm(POWER)
            pool.dma_start(base_tab[:, :, :, :], a["rope_1"].rearrange("(t p) a d -> p t a d", p=P)).then_inc(*start_loads["tab"].at(0))
            pool.dma_start(win_mask[:, :], a["window"]).then_inc(*start_loads["mask"].at(0))
            for layer in range(2):
                for name, col, n in (("diff_q_norm", 0, 32), ("diff_k_norm", 32, 32), ("gqa_q_norm", 64, 64),
                                     ("gqa_k_norm", 128, 64), ("nat_q_norm", 192, 64), ("nat_k_norm", 256, 64),
                                     ("diff_subln", SUBLN_AT, 64)):
                    pool.dma_start(gains[:, layer, col:col + n], a[name][layer:layer + 1, :].broadcast_to([P, n])) \
                        .then_inc(*start_loads["gains"].at((layer, name)))
            for i, name in enumerate(("lambda_q1", "lambda_k1", "lambda_q2", "lambda_k2")):
                for layer in range(2):
                    pool.dma_start(lam[:, i, layer, :], a[name][layer:layer + 1, :].broadcast_to([P, 32])) \
                        .then_inc(*start_loads["lambdas"].at((i, layer)))

            def bias_in_dram():
                pool.memset(far[:, :], NEG).then_inc(*setup_p.at("far"))
                pool.wait_ge(*setup_p.seen("far"))
                lines = 2 * C_HEADS * RPB_LINES
                pool.wait_ge(*projected.seen(("in0", 0, 3)))
                pool.dma_start(a["bias"], far[:, :].unsqueeze(1).broadcast_to([lines, GRID_W, BIAS_W])).then_inc(*bias_out.at("far"))
                for row in range(3):
                    pool.dma_start(ada_gate[:, row, :], a["b_ada"][row // 2:row // 2 + 1, 2 * D:3 * D].broadcast_to([P, D])) \
                        .then_inc(*start_loads["gate_bias"].at(row))

            def bias_lines():
                pool.wait_ge(*bias_out.seen("far"))
                for layer in range(2):
                    for h in range(C_HEADS):
                        dst = bass.AP(a["bias"].tensor, (layer * C_HEADS + h) * RPB_LINES * GRID_W * BIAS_W + 1,
                                      [[GRID_W * BIAS_W, RPB_LINES], [BIAS_W + 1, GRID_W], [1, RPB_W]])
                        src = a["nat_rpb"][layer, h, WIN_H - 4:WIN_H + 3, :].unsqueeze(1).broadcast_to([RPB_LINES, GRID_W, RPB_W])
                        pool.dma_start(dst, src).then_inc(*bias_out.at((layer, h)))

            def load_bias(layer):
                pool.wait_ge(*bias_out.seen((1, C_HEADS - 1)))
                for b in range(2):
                    for h in range(C_HEADS):
                        line = (layer * C_HEADS + h) * RPB_LINES + 1 - b
                        src = a["bias"][line:line + 6, :, WIN_W:WIN_W + GRID_W].rearrange("m q k -> q m k")
                        pool.dma_start(nat_bias[b * GRID_W:(b + 1) * GRID_W, h, :, :], src) \
                            .then_inc(*start_loads["bias"].at((layer, b, h)))

            def mask_bias(layer):
                pool.wait_ge(*start_loads["bias"].seen((layer, 1, C_HEADS - 1)))
                pool.wait_ge(*start_loads["mask"].seen(0))
                for h in range(C_HEADS):
                    ins = pool.tensor_tensor(nat_bias[:, h, :, :], nat_bias[:, h, :, :],
                                             win_mask[:, :].unsqueeze(1).broadcast_to([P, 6, GRID_W]), ALU.add)
                ins.then_inc(*bias_masked.at(layer))

            def power(out_ap, in_ap, n, scale, eps, done, key):
                pool.tensor_scalar(out_ap, in_ap, scale, eps, ALU.mult, ALU.add).then_inc(*means.at((done.name, key)))
                pool.wait_ge(*means.seen((done.name, key)))
                pool.tensor_tensor(out_ap, out_ap, half.broadcast_to([P, n]), ALU.pow).then_inc(*done.at(key))

            def norm(ph, tiles=None):
                for tt in tiles or tiles_of(ph):
                    pool.wait_ge(*squares.seen((ph, tt, 1)))
                    pool.tensor_tensor(sm(RS + tt), sm(SS + 2 * tt), sm(SS + 2 * tt + 1), ALU.add).then_inc(*rstd.at((ph, tt, "sum")))
                    pool.wait_ge(*rstd.seen((ph, tt, "sum")))
                    power(sm(RS + tt), sm(RS + tt), 1, 1.0 / D, EPS, rstd, (ph, tt))

            def make_tabs(layer):
                pool.wait_ge(*start_loads["tab"].seen(0))
                pool.wait_ge(*setup_v.seen("q_gains"))
                for tt in range(2):
                    for q in range(2):
                        for at, d, g in ((0, 32, 0), (32, 64, 64)):
                            g = gains[:, layer, g + q * d:g + (q + 1) * d]
                            o1, o2 = tab(tt, q, 0, at, d), tab(tt, q, 1, at, d)
                            h = d // 2
                            cos, sin, minus_sin = (base_tab[:, tt, i, at // 2:at // 2 + h] for i in range(3))
                            pool.tensor_tensor(o1.rearrange("p (a h) -> p a h", a=2), g.rearrange("p (a h) -> p a h", a=2),
                                               cos.unsqueeze(1).broadcast_to([P, 2, h]), ALU.mult)
                            pool.tensor_tensor(o2[:, 0:h], minus_sin, g[:, h:d], ALU.mult)
                            ins = pool.tensor_tensor(o2[:, h:d], sin, g[:, 0:h], ALU.mult)
                ins.then_inc(*tabs_made.at(layer))

            def process_in(ph, c, stages):
                tts = tiles_of(ph)
                if c not in CHUNK_HEADS:
                    return
                for k in stages:
                    if 1 <= k <= len(tts) and c in (0, 2) and tts[k - 1] in X_TILES:
                        tt = tts[k - 1]
                        pool.wait_ge(*head_scaled.seen((ph, c, tt)))
                        if tt == 1:
                            pool.wait_ge(*heads_made.seen((ph, c, 0)))
                        for col, w, d, name, q in CHUNK_HEADS[c]:
                            ins = rope_product(pool, swapped[0][:, col:col + w], stage, 512 * tt + col, STAGE_W, w, d,
                                               tab(tt, q, 1, 0 if name == "A" else 32, d))
                        ins.then_inc(*rope_b.at((ph, c, tt)))
                    if k < len(tts):
                        u = (ph, c, tts[k])
                        d = CHUNK_HEADS[c][0][2]
                        n = head_span(*u)[1] // d
                        pool.wait_ge(*head_sum.seen(u))
                        power(rs_of(tts[k] % 2, n), ss_of(tts[k] % 2, n), n, 1.0 / d, EPS, head_rstd, u)

            def project_in(ph):
                for c in range(7):
                    for n in range(4):
                        process_in(ph, c - 1, (n + 2,))
                        if n == 3:
                            process_in(ph, c, (0, 1))
                        if (ph, c, n) == ("in0", 1, 3):
                            bias_lines()
                        if (ph, c, n) == ("in0", 3, 3):
                            load_bias(0)

            def diff_norm(layer):
                for qt in (ALL_TILES if layer == 0 else X_TILES):
                    pool.wait_ge(*y_made.seen((layer, qt, "A", A_HEADS - 1)))
                    pool.wait_ge(*diff_sum.seen((layer, qt, A_HEADS - 1)))
                    power(sm(DIFF_RS + 4 * qt, 4), sm(DIFF_SS + 4 * qt, 4), 4, 1.0 / HD, EPS, diff_rstd, (layer, qt))
                    y = gate[:, qt, 0:256].rearrange("p (h d) -> p h d", d=HD)
                    sub = gains[:, layer, SUBLN_AT:SUBLN_AT + HD].unsqueeze(1).broadcast_to([P, A_HEADS, HD])
                    pool.tensor_tensor(y, y, sub, ALU.mult).then_inc(*diff_normed.at((layer, qt, "gain")))
                    pool.wait_ge(*diff_normed.seen((layer, qt, "gain")))
                    pool.wait_ge(*diff_rstd.seen((layer, qt)))
                    pool.tensor_tensor(y, y, sm(DIFF_RS + 4 * qt, 4).unsqueeze(2).broadcast_to([P, A_HEADS, HD]), ALU.mult) \
                        .then_inc(*diff_normed.at((layer, qt)))

            norm("in0")
            make_tabs(0)
            bias_in_dram()
            project_in("in0")
            mask_bias(0)
            diff_norm(0)
            pool.wait_ge(*heads_made.seen(("in0", 5, 3)))
            make_tabs(1)
            pool.wait_ge(*y_made.seen(units_of(0)[-1]))
            load_bias(1)
            mask_bias(1)
            norm("in1")
            project_in("in1")
            diff_norm(1)
            norm("gin")
            pool.wait_ge(*out_scaled.seen(("out1", 1, 1)))
            pool.dma_start(ws_raw[:, :, :], a["a_w_s_2"][0].rearrange("g t s -> t g s")).then_inc(*start_loads["ws"].at(0))
            pool.dma_start(ln_gb[:, 0, :], a["a_ln_g_2"].broadcast_to([P, GMLP])).then_inc(*start_loads["ln"].at(0))
            pool.dma_start(ln_gb[:, 1, :], a["a_ln_b_2"].broadcast_to([P, GMLP])).then_inc(*start_loads["ln"].at(1))
            pool.dma_start(post_gain, a["norm_post_2"][0:1, :].broadcast_to([P, D])).then_inc(*start_loads["post"].at(0))
            pool.dma_start(dil_mask, a["dil_mask"]).then_inc(*start_loads["dil_mask"].at(0))
            pool.dma_start(tabs[:, 0:512].rearrange("p (t a) -> p t a", t=2), a["rope_2"].rearrange("(t p) a -> p t a", p=P)) \
                .then_inc(*start_loads["dil_tab"].at(0))
            pool.wait_ge(*start_loads["ws"].seen(0))
            pool.affine_select(out=ws_raw[:, :, :], in_=ws_raw[:, :, :], compare_op=ALU.is_ge, fill=0.0, base=0,
                               pattern=[[0, GROUPS], [-1, P]], channel_multiplier=1).then_inc(*setup_p.at("ws"))
            for tt in X_TILES:
                pool.wait_ge(*stats.seen(("aggr", tt)))
                power(sm(LN_RS + tt), sm(LN_MV + 2 * tt + 1), 1, 1.0, LN_EPS, rstd, ("ln", tt))
                pool.wait_ge(*ln_v.seen((tt, "gain")))
                pool.tensor_tensor(gv[:, tt, :], gv[:, tt, :], ln_gb[:, 1, :], ALU.add).then_inc(*ln_p.at(tt))

            def post(ph):
                for tt in X_TILES:
                    if ph == "gout" and tt:
                        norm("din", (0,))
                    pool.wait_ge(*values_kept.seen((ph, 1, tt)))
                    pool.tensor_tensor(sm(POST_SUM + tt), sm(POST_SS + 2 * tt), sm(POST_SS + 2 * tt + 1), ALU.add) \
                        .then_inc(*post_sum.at((ph, tt)))
                    pool.wait_ge(*post_sum.seen((ph, tt)))
                    power(sm(POST_RS + tt), sm(POST_SUM + tt), 1, 1.0 / D, EPS, rstd, (ph, tt))

            post("gout")
            norm("din", (1,))
            pool.wait_ge(*added.seen(("gout", 1, 1)))
            pool.dma_start(post_gain, a["norm_post_2"][1:2, :].broadcast_to([P, D])).then_inc(*start_loads["post"].at(1))
            for c in range(20):
                for tt in X_TILES:
                    u = ("din", c, tt)
                    if head_span(*u):
                        pool.wait_ge(*dil_rope.seen(u))
                        t = heads[turn_slot(*u)]
                        pool.tensor_tensor(t, t, swapped[tt], ALU.add).then_inc(*dil_heads_made.at(u))
            post("dout")

        @block.vector
        def _(dve):
            at = [0]

            def split_until(n):
                for i in range(at[0], min(n, len(SPLITS))):
                    p = SPLITS[i]
                    dve.wait_ge(*weights_hi.seen(p))
                    dve.tensor_tensor(w_lo[:, i % SPLIT, :, :], raw[:, PIECE_AT[p] % RAW, :, :],
                                      w_hi[:, i % SPLIT, :, :].bitcast(F32), ALU.subtract).then_inc(*weights_lo.at(p))
                at[0] = max(at[0], n)

            def ada_products(p):
                name, j, pair = p
                slot = PIECE_AT[p] % RAW
                dve.wait_ge(*landed[slot].seen(p))
                first = 1 if ada_at_start(name, j) else 0
                if pair == first:
                    before = (("ada0", j - 2) if j >= 2 else None) if ada_at_start(name, j) else \
                        {("ada0", 4): None, ("ada0", 5): ("ada0", 4, 1), ("ada1", 0): ("ada0", 5, 1), ("ada1", 5): ("ada1", 4, 0)}.get((name, j), (name, j - 1))
                    if before:
                        dve.wait_ge(*ada_summed.seen(before))
                for k in range(2):
                    for who in ada_whos(name, j):
                        to, w, c = ada_place(name, j)[:, who, :], raw[:, slot, k, :], cvec[:, 2 * pair + k, who:who + 1]
                        if pair == first and k == 0:
                            dve.tensor_scalar(to, w, c, None, ALU.mult).then_inc(*ada_vector.at((*p, k, who)))
                            continue
                        dve.wait_ge(*ada_vector.seen((*p, 0, who) if k else (name, j, pair - 1, 1, who)))
                        dve.scalar_tensor_tensor(to, w, c, to, ALU.mult, ALU.add).then_inc(*ada_vector.at((*p, k, who)))

            def ada_keep(name, j):
                layer = int(name[3])
                if j < 4:
                    b = 56 + 24 * layer + 4 * j
                    dve.wait_ge(*ada_summed.seen((name, j)))
                    dve.tensor_tensor(ada_cols[:, 4 * j:4 * j + 4, :], bank_of("ada", name, j)[:, 0:8].rearrange("p (k w) -> p k w", w=2),
                                      cols[:, b:b + 4].unsqueeze(2).broadcast_to([P, 4, 2]), ALU.add).then_inc(*ada_kept.at((name, j)))
                if j == 3:
                    g = cols[:, 16 + 8 * layer:24 + 8 * layer].unsqueeze(2).broadcast_to([P, KT, 2])
                    dve.wait_ge(*ada_kept.seen((name, j)))
                    dve.scalar_tensor_tensor(a_scale[:, :, :], ada_cols[:, 8:16, :], 1.0, g, ALU.add, ALU.mult) \
                        .then_inc(*ada_scale_made.at(f"in{layer}"))
                if j >= 4:
                    dve.wait_ge(*start_loads["gate_bias"].seen(2))
                    for who in ada_whos(name, j):
                        to = ada_gate[:, 2 * layer + who, (j - 4) * NC:(j - 3) * NC]
                        dve.wait_ge(*ada_summed.seen((name, j, who)))
                        dve.tensor_tensor(to, to, bank_of("ada", name, j, who)[:, :], ALU.add).then_inc(*ada_kept.at((name, j, who)))

            def normalise(ph, tt):
                dve.wait_ge(*rstd.seen((ph, tt)))
                if tt >= 2:
                    dve.wait_ge(*tpose.seen((ph, tt - 2, 1)))
                dve.tensor_scalar(xn[tt % 2], x[:, tt, :], sm(RS + tt), None, ALU.mult).then_inc(*normed.at((ph, tt)))

            def norm_tile(ph, tt):
                bias = ph in ("in0", "in1")
                v = vt[tt % 2]
                who = 0 if tt in X_TILES else 1
                dve.wait_ge(*tpose.seen((ph, tt, 0)))
                if bias and tt == 0:
                    dve.wait_ge(*ada_scale_made.seen(ph))
                for i in range(4):
                    src, dst = bank_of("norm", ph, tt, 0)[:, i * P:(i + 1) * P], v[:, i * P:(i + 1) * P]
                    if bias:
                        ins = dve.tensor_scalar(dst, src, norm_scale(ph, i, who), ada_cols[:, i, who:who + 1], ALU.mult, ALU.add)
                    else:
                        ins = dve.tensor_scalar(dst, src, norm_scale(ph, i, who), None, ALU.mult)
                ins.then_inc(*scaled_v.at((ph, tt)))
                if tt + 2 in tiles_of(ph):
                    normalise(ph, tt + 2)
                for half in range(2):
                    dve.wait_ge(*h_hi_made.seen((ph, tt, half)))
                    hi = hT4(h_hi, ph, half * 4, tt).bitcast(F32)
                    dve.tensor_tensor(hT4(h_lo, ph, half * 4, tt), v[:, half * 512:(half + 1) * 512].rearrange("p (k t) -> p k t", k=4),
                                      hi, ALU.subtract).then_inc(*h_lo_made.at((ph, tt, half)))

            def end_of(ph, process_tile):
                following, tts = FOLLOWING[ph], tiles_of(ph)
                first = SPLIT_AT[(following, 0, 0)]
                for tt in tts[:-1]:
                    process_tile(ph, 1, tt)
                    if tt:
                        normalise(following, tt - 1)
                if len(tts) == 2:
                    normalise(following, 0)
                if len(tts) == 4:
                    norm_tile(following, 0)
                split_until(first + SPLIT - 1)
                if len(tts) == 2:
                    norm_tile(following, 0)
                process_tile(ph, 1, tts[-1])
                split_until(first + SPLIT)
                if len(tts) == 2:
                    normalise(following, 1)
                for tt in tiles_of(following)[1:]:
                    norm_tile(following, tt)

            def y_part(ph, tt, q):
                dve.wait_ge(*h_hi_made.seen((ph, tt, q)))
                src = bank_of("y", ph, tt, q)[:, :].rearrange("p (k t) -> p k t", k=4)
                dve.tensor_tensor(hT4(h_lo, ph, q * 4, tt), src, hT4(h_hi, ph, q * 4, tt).bitcast(F32), ALU.subtract) \
                    .then_inc(*h_lo_made.at((ph, tt, q)))

            def project(ph, process, after_piece=None):
                pairs = PROJ[ph][1] // 2
                limit = SPLIT_AT[(ph, 0, 0)] + PROJ[ph][0] * pairs if ph == "in0" else len(SPLITS)
                for c in range(PROJ[ph][0] - (1 if FOLLOWING.get(ph) and pairs <= SPLIT else 0)):
                    for n in range(pairs):
                        p = (ph, c, n)
                        if ph in FOLLOWING and c == PROJ[ph][0] - 1 and n >= pairs - SPLIT:
                            continue
                        if after_piece:
                            after_piece((p, 0))
                        if ph in ("in0", "in1"):
                            process(ph, c - 1, (n + 2,))
                        if n < pairs - 1:
                            split_until(min(limit, SPLIT_AT[p] + SPLIT + 1))
                        if p in ADA_READY:
                            ada_keep(*ADA_READY[p])
                        if p in ADA_BESIDE:
                            ada_products(ADA_BESIDE[p])
                        if after_piece:
                            after_piece((p, 1))
                        if n == pairs - 1:
                            split_until(min(limit, SPLIT_AT[p] + SPLIT + (1 if ph in FOLLOWING else 0)))
                            process(ph, c)
                            split_until(min(limit, SPLIT_AT[p] + SPLIT + 1))

            def process_in(ph, c, stages=(0, 1)):
                if c not in CHUNK_HEADS:
                    return
                layer = int(ph[2])
                d = CHUNK_HEADS[c][0][2]

                def sum_squares(tt):
                    u = (ph, c, tt)
                    lo, w = head_span(*u)
                    dve.wait_ge(*head_sq.seen(u))
                    dve.tensor_reduce(ss_of(tt % 2, w // d), sq[:, lo:lo + w].rearrange("p (n d) -> p n d", d=d), AX, ALU.add) \
                        .then_inc(*head_sum.at(u))

                def scale(tt):
                    u = (ph, c, tt)
                    lo, w = head_span(*u)
                    t = heads[tt][:, lo:lo + w].rearrange("p (n d) -> p n d", d=d)
                    dve.wait_ge(*head_rstd.seen(u))
                    dve.tensor_tensor(t, t, rs_of(tt % 2, w // d).unsqueeze(2).broadcast_to([P, w // d, d]), ALU.mult) \
                        .then_inc(*head_scaled.at(u))

                def finish(tt):
                    u = (ph, c, tt)
                    lo, w = head_span(*u)
                    rope = c in (0, 2) and tt in X_TILES
                    dve.wait_ge(*head_scaled.seen(u))
                    if rope:
                        dve.wait_ge(*tabs_made.seen(layer))
                        dve.wait_ge(*rope_b.seen(u))
                    for col, w_, _, name, q in CHUNK_HEADS[c]:
                        k = kept_columns(ph, c, tt, col, w_)
                        if not k:
                            continue
                        t = heads[tt][:, k[0]:k[0] + k[1]].rearrange("p (n d) -> p n d", d=d)
                        g = tab(tt, q, 0, 0 if name == "A" else 32, d) if rope else \
                            gains[:, layer, GAIN_AT[name][q]:GAIN_AT[name][q] + d]
                        ins = dve.tensor_tensor(t, t, g.unsqueeze(1).broadcast_to([P, k[1] // d, d]), ALU.mult)
                    if rope:
                        ins.then_inc(*rope_a.at(u))
                        dve.wait_ge(*rope_a.seen(u))
                        t = heads[tt][:, lo:lo + w]
                        ins = dve.tensor_tensor(t, t, swapped[0][:, lo:lo + w], ALU.add)
                    ins.then_inc(*heads_made.at(u))

                tts = tiles_of(ph)
                for k in stages:
                    if k < len(tts):
                        sum_squares(tts[k])
                    if 1 <= k <= len(tts):
                        scale(tts[k - 1])
                    if k >= 2:
                        finish(tts[k - 2])

            def out_tile(ph, c, tt):
                u = (ph, c, tt)
                who = 2 if ph == "out1" else 0 if tt in X_TILES else 1
                dve.wait_ge(*projected.seen(u))
                dve.tensor_tensor(out_part[tt % 2], bank_of("proj", *u)[:, :], ada_gate[:, who, c * NC:(c + 1) * NC], ALU.mult) \
                    .then_inc(*out_scaled.at(u))
                dve.wait_ge(*out_scaled.seen(u))
                dve.tensor_tensor(x[:, tt, c * NC:(c + 1) * NC], x[:, tt, c * NC:(c + 1) * NC], out_part[tt % 2], ALU.add) \
                    .then_inc(*added.at(u))

            def process_out(ph, c):
                for tt in tiles_of(ph):
                    out_tile(ph, c, tt)

            def attention1(layer):
                units = units_of(layer)
                fill = fill_of(layer)

                def unit_max(u):
                    _, qt, kind, h = u
                    k0 = 0 if qt in X_TILES else 256
                    for m in range(2 if kind == "A" else 1):
                        n = prob_at[(u, m)]
                        bank = bank_of("score", layer, n)
                        dve.wait_ge(*scores.seen((u, m)))
                        if kind == "C" and qt in X_TILES:
                            dve.tensor_reduce(sm(NM1 + n % 4), bank[:, 256:512], AX, ALU.max, negate=True).then_inc(*row_max.at((u, "ctx")))
                            dve.wait_ge(*row_max.seen((u, "ctx")))
                            dve.wait_ge(*bias_masked.seen(layer))
                            if n >= 4:
                                dve.wait_ge(*prob_free(layer, n - 4))
                            near = nat_bias[:, h, 2 - 2 * qt:6 - 2 * qt, :].rearrange("p m k -> p (m k)")
                            dve.tensor_tensor_reduce(probs[n % 4][:, 0:256], bank[:, 0:256], near, -1.0, sm(NM1 + n % 4),
                                                     ALU.add, ALU.min, nm_col(u, m)).then_inc(*row_max.at((u, m)))
                        else:
                            dve.tensor_reduce(nm_col(u, m), bank[:, k0:512], AX, ALU.max, negate=True).then_inc(*row_max.at((u, m)))

                def weigh(u):
                    _, qt, kind, h = u
                    k0 = 0 if qt in X_TILES else 256
                    n = prob_at[(u, 0)]
                    rz = sm(RZ + n % 8)
                    if kind == "A":
                        z0 = z_col(u, 0)[0]
                        dve.wait_ge(*exps.seen((layer, n + 1)))
                        dve.reciprocal(sm(RZ + n % 8, 2), sm(Z + 2 * (n % 4), 4).rearrange("p (m z) -> p m z", z=2)[:, :, 0]) \
                            .then_inc(*recips.at((u, "both")))
                        dve.wait_ge(*recips.seen((u, "both")))
                        dve.tensor_scalar(sm(NM1 + 4), sm(RZ + n % 8 + 1), sm(NLAM + layer), z0, ALU.mult, ALU.mult).then_inc(*recips.at(u))
                        dve.wait_ge(*recips.seen(u))
                        p0, p1 = probs[n % 4][:, k0:512], probs[(n + 1) % 4][:, k0:512]
                        dve.scalar_tensor_tensor(p0, p1, sm(NM1 + 4), p0, ALU.mult, ALU.add).then_inc(*weighed.at(u))
                    elif kind == "C" and qt in X_TILES:
                        dve.wait_ge(*exps.seen((layer, n)))
                        dve.tensor_tensor(z_col(u, 0)[0], z_col(u, 0)[0], z_col(u, 0)[1], ALU.add).then_inc(*weighed.at(u))
                        dve.wait_ge(*weighed.seen(u))
                        dve.reciprocal(rz, z_col(u, 0)[0]).then_inc(*recips.at(u))
                    else:
                        dve.wait_ge(*exps.seen((layer, n)))
                        dve.reciprocal(rz, z_col(u, 0)[0]).then_inc(*recips.at(u))

                def output(u):
                    _, qt, kind, h = u
                    dve.wait_ge(*attended.seen(u))
                    if kind == "A":
                        dve.wait_ge(*diff_sum.seen((layer, qt, h)))
                    dve.wait_ge(*recips.seen(u))
                    col = {"A": 0, "B": 256, "C": 640}[kind] + h * HD
                    g = gate[:, qt, col:col + HD]
                    dve.scalar_tensor_tensor(g, head_output(u), sm(RZ + prob_at[(u, 0)] % 8), g, ALU.mult, ALU.mult) \
                        .then_inc(*y_made.at(u))

                def step(i):
                    if i == 0:
                        unit_max(units[0])
                    if i + 1 < len(units):
                        unit_max(units[i + 1])
                    if i < len(units):
                        weigh(units[i])
                    tasks = fill.get(i, ())
                    for task in tasks:
                        if task[0] == "ada":
                            ada_keep(*task[1:])
                    if i >= 2:
                        output(units[i - 2])
                    for task in tasks:
                        if task[0] == "products":
                            ada_products(task[1])
                        if task[0] == "y":
                            y_part(f"out{layer}", task[1], 0)
                        if task[0] == "split":
                            split_until(SPLIT_AT[(f"out{layer}", 0, 0)] + task[1] + 1)

                return step, len(steps_beside(f"in{layer}")), len(units)

            def project_with(ph, process, attention):
                step, solo, units = attention
                slots = steps_beside(ph)
                project(ph, process, lambda p: step(slots[p]) if p in slots else None)
                for i in range(solo, units + 2):
                    step(i)

            dve.wait_ge(*setup_t.seen("rows"))
            dve.tensor_copy(cols[:, :], bank_of("rows")[:, 0:ROWS]).then_inc(*setup_v.at("cols"))
            dve.wait_ge(*setup_a.seen("cvec"))
            for j in range(4):
                for pair in range(1, 4):
                    ada_products(("ada0", j, pair))
                if j:
                    ada_keep("ada0", j - 1)
            for tt in X_TILES:
                normalise("in0", tt)
            dve.wait_ge(*start_loads["lambdas"].seen((3, 1)))
            for layer in range(2):
                for i in range(2):
                    ins = dve.tensor_tensor_reduce(st(5120 + 32 * (2 * layer + i), 32), lam[:, 2 * i, layer, :], lam[:, 2 * i + 1, layer, :],
                                                   1.0, 0.0, ALU.mult, ALU.add, sm(LAM_SUM + 2 * layer + i))
            ins.then_inc(*setup_v.at("lambda_sums"))
            dve.wait_ge(*start_loads["gains"].seen((1, "diff_subln")))
            for layer in range(2):
                lam_init = 0.8 - 0.6 * math.exp(-0.3 * layer)
                for col, n, f in ((0, 32, 32 ** -0.5), (64, 64, HD ** -0.5), (192, 64, HD ** -0.5), (SUBLN_AT, 64, 1 - lam_init)):
                    g = gains[:, layer, col:col + n]
                    ins = dve.tensor_scalar(g, g, f, None, ALU.mult)
            ins.then_inc(*setup_v.at("q_gains"))
            ada_keep("ada0", 3)
            norm_tile("in0", 0)
            split_until(SPLIT)
            for tt in ALL_TILES[1:]:
                norm_tile("in0", tt)
            dve.wait_ge(*setup_a.seen("lambda_exp"))
            for layer in range(2):
                lam_init = 0.8 - 0.6 * math.exp(-0.3 * layer)
                e1, e2 = sm(LAM_EXP + 2 * layer), sm(LAM_EXP + 2 * layer + 1)
                dve.tensor_tensor(sm(NLAM + layer), e2, e1, ALU.subtract).then_inc(*setup_v.at(("lam", layer)))
                dve.wait_ge(*setup_v.seen(("lam", layer)))
                dve.tensor_scalar(sm(NLAM + layer), sm(NLAM + layer), -lam_init, None, ALU.add).then_inc(*setup_v.at(("nlam", layer)))
            project_with("in0", process_in, attention1(0))
            for tt in ALL_TILES:
                y_part("out0", tt, 1)
            project("out0", process_out)
            end_of("out0", out_tile)
            project_with("in1", process_in, attention1(1))
            for tt in X_TILES:
                y_part("out1", tt, 1)
            project("out1", process_out)
            end_of("out1", out_tile)

            def process_gin(ph, c):
                if c < 4:
                    for tt in X_TILES:
                        dve.wait_ge(*values_kept.seen((ph, c, tt)))
                        dve.bn_stats(sm(STATS + 24 * tt + 6 * c, 6), gv[:, tt, c * NC:(c + 1) * NC]).then_inc(*stats.at((c, tt)))
                if c == 3:
                    for tt in X_TILES:
                        dve.wait_ge(*stats.seen((c, tt)))
                        dve.bn_aggr(sm(LN_MV + 2 * tt, 2), sm(STATS + 24 * tt, 24)).then_inc(*stats.at(("aggr", tt)))
                if 6 <= c <= 9:
                    j = c - 6
                    for tt in X_TILES:
                        dve.wait_ge(*spatial.seen((j, tt)))
                        for i in range(2):
                            g = 2 * j + i
                            bank = bank_of("spatial", j, tt)
                            u = gu[:, tt, g * 256:(g + 1) * 256]
                            ins = dve.scalar_tensor_tensor(u, bank[:, i * 256:(i + 1) * 256], cols[:, 48 + g:49 + g], u, ALU.add, ALU.mult)
                        ins.then_inc(*gated.at((j, tt)))
                if c >= 8:
                    for tt in X_TILES:
                        dve.wait_ge(*values_kept.seen((ph, c, tt)))
                        u = gu[:, tt, (c - 8) * NC:(c - 7) * NC]
                        dve.tensor_tensor(u, u, silu_z[((c - 8) * 2 + tt) % 4], ALU.mult).then_inc(*gated.at(("z", c - 8, tt)))

            def layer_norm(place):
                p, k = place
                if p[1] != 4 or k == 0:
                    return
                tt = p[2] // 2
                if p[2] % 2 == 0:
                    dve.wait_ge(*rstd.seen(("ln", tt)))
                    dve.tensor_scalar(gv[:, tt, :], gv[:, tt, :], sm(LN_MV + 2 * tt), sm(LN_RS + tt), ALU.subtract, ALU.mult) \
                        .then_inc(*ln_v.at((tt, "scaled")))
                else:
                    dve.wait_ge(*start_loads["ln"].seen(1))
                    dve.wait_ge(*ln_v.seen((tt, "scaled")))
                    dve.tensor_tensor(gv[:, tt, :], gv[:, tt, :], ln_gb[:, 0, :], ALU.mult).then_inc(*ln_v.at((tt, "gain")))

            project("gin", process_gin, layer_norm)
            for q in range(4):
                for tt in X_TILES:
                    y_part("gout", tt, q)

            def post_tile(ph, c, tt):
                if c == 0:
                    return
                dve.wait_ge(*start_loads["post"].seen(0 if ph == "gout" else 1))
                dve.wait_ge(*rstd.seen((ph, tt)))
                dve.scalar_tensor_tensor(y_out[:, tt, :], y_out[:, tt, :], sm(POST_RS + tt), post_gain, ALU.mult, ALU.mult) \
                    .then_inc(*post_v.at((ph, tt)))
                dve.wait_ge(*post_v.seen((ph, tt)))
                dve.tensor_tensor(x[:, tt, :], x[:, tt, :], y_out[:, tt, :], ALU.add).then_inc(*added.at((ph, 1, tt)))

            project("gout", lambda ph, c: None)
            end_of("gout", post_tile)
            dve.wait_ge(*start_loads["dil_tab"].seen(0))
            dve.wait_ge(*start_loads["dil_mask"].seen(0))

            def process_din(ph, c):
                for tt in X_TILES:
                    u = (ph, c, tt)
                    if not head_span(*u):
                        continue
                    q = (DIN_COLS[c] // 2) % 3
                    bank = bank_of("proj", *u)
                    dve.wait_ge(*projected.seen(u))
                    before = step_before(u, 4)
                    if before:
                        dve.wait_ge(*tpose.seen(("heads", *before)))
                    t = tt * 256 + q * 128
                    dve.tensor_tensor(heads[turn_slot(*u)].rearrange("p (n d) -> p n d", d=HD), bank[:, :].rearrange("p (n d) -> p n d", d=HD),
                                      tabs[:, t:t + HD].unsqueeze(1).broadcast_to([P, 8, HD]), ALU.mult)
                    before = step_before(u, 2)
                    if before:
                        dve.wait_ge(*made_heads(before))
                    rope_product(dve, swapped[tt], bank, 0, 512, NC, HD, tabs[:, t + HD:t + 2 * HD]).then_inc(*dil_rope.at(u))

            def dil_max(i):
                qt = i % 2
                nk = (qt + 1) * P
                dve.wait_ge(*scores.seen(("dil", i)))
                if i >= 3:
                    dve.wait_ge(*probs_turned.seen(("dil", i - 3, (i - 3) % 2)))
                mask = dil_mask[:, :, 2 * P - nk:2 * P]
                to = probs2[i % 3]
                bank = bank_of("dscore", i, 0)
                if qt == 0:
                    dve.tensor_tensor_reduce(to[:, 0:384].rearrange("p (g k) -> p g k", g=3), bank[:, 0:384].rearrange("p (g k) -> p g k", g=3),
                                             mask, -1.0, -NEG, ALU.add, ALU.min, sm(DNM + i % 4)).then_inc(*row_max.at(("dil", i)))
                else:
                    dve.tensor_tensor_reduce(to[:, 0:512].rearrange("p (g k) -> p g k", g=2), bank[:, 0:512].rearrange("p (g k) -> p g k", g=2),
                                             mask[:, 0:2, :], -1.0, -NEG, ALU.add, ALU.min, sm(NM1)).then_inc(*row_max.at(("dil", i, 0)))
                    dve.wait_ge(*row_max.seen(("dil", i, 0)))
                    dve.tensor_tensor_reduce(to[:, 512:768], bank_of("dscore", i, 1)[:, 0:256], mask[:, 2, :], -1.0, sm(NM1), ALU.add, ALU.min,
                                             sm(DNM + i % 4)).then_inc(*row_max.at(("dil", i)))

            def dil_step(i):
                if i == 0:
                    dil_max(0)
                if i < 31:
                    dil_max(i + 1)
                j = i - 2
                if j >= 0:
                    qt, h = j % 2, j // 2
                    dve.wait_ge(*exps.seen(("dil", j)))
                    dve.reciprocal(sm(DRZ + j % 4), sm(DZ + j % 4)).then_inc(*recips.at(("dil", j)))
                    dve.wait_ge(*recips.seen(("dil", j)))
                    dve.wait_ge(*attended.seen(("dil", j)))
                    g = dgate[:, qt, h * HD:(h + 1) * HD]
                    dve.scalar_tensor_tensor(g, bank_of("dout", j)[:, h % 2 * HD:(h % 2 + 1) * HD], sm(DRZ + j % 4), g, ALU.mult, ALU.mult) \
                        .then_inc(*y_made.at(("dil", j)))

            project_with("din", process_din, (dil_step, len(steps_beside("din")), 32))
            for tt in X_TILES:
                for q in range(2):
                    y_part("dout", tt, q)
            project("dout", lambda ph, c: None)
            for tt in X_TILES:
                post_tile("dout", 1, tt)

    return {name: c.found for name, c in counts.items()}


_INS = ['x', 'c', 'ctx', 'c_ctx', 'norm_g', 'w_ada', 'b_ada', 'w_in', 'w_out', 'diff_q_norm', 'diff_k_norm',
        'lambda_q1', 'lambda_k1', 'lambda_q2', 'lambda_k2', 'diff_subln', 'gqa_q_norm', 'gqa_k_norm', 'nat_q_norm',
        'nat_k_norm', 'nat_rpb', 'norm_pre_2', 'norm_post_2', 'a_w_in_2', 'a_ln_g_2', 'a_ln_b_2', 'a_w_s_2',
        'a_b_s_2', 'a_w_out_2', 'b_w_in_2', 'b_w_out_2']


def _constants():
    t = np.arange(SEQ)
    row, col = (t // GRID_W).astype(np.float32), (t % GRID_W).astype(np.float32)
    parts = []
    for d in (32, HD):
        nf = d // 4
        inv = (np.float32(10000.0) ** (-np.arange(nf, dtype=np.float32) / np.float32(nf))).astype(np.float32)
        ang = np.concatenate([row[:, None] * inv, col[:, None] * inv], axis=-1)
        c, s = np.cos(ang), np.sin(ang)
        parts.append((c, s, -s))
    rope_1 = np.stack([np.concatenate([p[i] for p in parts], 1) for i in range(3)], 1).astype(np.float32)
    inv = (1.0 / (np.float32(10000.0) ** (np.arange(0, HD, 2, dtype=np.float32) / np.float32(HD)))).astype(np.float32)
    ang = t.astype(np.float32)[:, None] * inv[None, :]
    c, s = np.cos(ang), np.sin(ang)
    c2, s2 = np.concatenate([c, c], 1), np.concatenate([-s, s], 1)
    f = HD ** -0.5
    rope_2 = np.concatenate([c2 * f, s2 * f, c2, s2], 1).astype(np.float32)
    q = (np.arange(P) % GRID_W)[:, None]
    k = np.arange(GRID_W)[None, :]
    first = np.clip(q - WIN_W // 2, 0, GRID_W - WIN_W)
    window = np.where((k >= first) & (k < first + WIN_W), 0.0, NEG).astype(np.float32)
    rel = P + np.arange(P)[:, None] - np.arange(SEQ)[None, :]
    dil = [np.where((rel >= 0) & (rel % r == 0) & (rel <= w), 0.0, NEG) for w, r in ((128, 1), (512, 4), (2048, 16))]
    return {"rope_1": rope_1, "rope_2": rope_2, "window": window, "dil_mask": np.stack(dil, 1).astype(np.float32)}


def kernel(**inputs):
    import concourse.bacc as _bacc
    from concourse.bass_utils import run_bass_kernel_spmd as _run

    arrays = {f"in_{n}_dram": np.ascontiguousarray(inputs[n]) for n in _INS}
    arrays.update({f"in_{n}_dram": v for n, v in _constants().items()})

    def build(known):
        nc = _bacc.Bacc("TRN2", target_bir_lowering=False, num_devices=1)
        a = {n[3:-5]: nc.dram_tensor(n, v.shape, F32, kind="ExternalInput").ap() for n, v in arrays.items()}
        a["bias"] = nc.dram_tensor("bias", (2 * C_HEADS * RPB_LINES, GRID_W, BIAS_W), F32).ap()
        out = nc.dram_tensor("out_0_dram", (1, SEQ, D), F32, kind="ExternalOutput").ap()
        return nc, first_then_second_block(nc, a, out, known)

    _, known = build(None)
    nc, _ = build(known)
    r = _run(nc, [arrays], core_ids=[0])
    return r.results[0]["out_0_dram"]
```
